# Optimizing a Trainium2 kernel written in Bass

```python
import jax, jax.numpy as jnp
from jax import lax
import numpy as np

D_MODEL = 1024
BATCH = 1
SEQ = 1024
DEPTH = 2
DEC_BATCH = 8
DEC_SEQ = 1
PAST_LEN = 4096
PAGE_SIZE = 128

HEAD_DIM = 64
N_Q_HEADS = 8
N_KV_HEADS = 2
Q_PER_KV = N_Q_HEADS // N_KV_HEADS
ATTN_DIM = N_Q_HEADS * HEAD_DIM
KV_DIM = N_KV_HEADS * HEAD_DIM
CONV_GROUPS = 8
CONV_DIM = CONV_GROUPS * HEAD_DIM
MIX_DIM = ATTN_DIM + CONV_DIM
IN_DIM = ATTN_DIM + 2 * KV_DIM + 3 * CONV_DIM
WINDOW = 128
ATTN_BLOCK = 128
CONV_K = 3
ROPE_THETA = 10000.0
N_GROUPS = 4
EXPERTS_PER_GROUP = 8
N_EXPERTS = N_GROUPS * EXPERTS_PER_GROUP
TOP_K = 2
D_EXPERT = 512
MOE_BLOCK = 256
LN_EPS = 1e-5
DEEPNORM_ALPHA = (2 * DEPTH) ** 0.25
DEEPNORM_BETA = (8 * DEPTH) ** -0.25

kernel_name = 'hymba_swa_sinkconv_hmoe_step'

def layer_norm(x, g, b):
    xf = x.astype(jnp.float32)
    mu = xf.mean(-1, keepdims=True)
    var = jnp.square(xf - mu).mean(-1, keepdims=True)
    return ((xf - mu) * lax.rsqrt(var + LN_EPS) * g + b).astype(x.dtype)

def rope(x, pos):
    half = HEAD_DIM // 2
    inv = ROPE_THETA ** (-jnp.arange(half, dtype=jnp.float32) / half)
    ang = pos.astype(jnp.float32)[:, None] * inv[None, :]
    cos = jnp.cos(ang)[:, None, :]
    sin = jnp.sin(ang)[:, None, :]
    x1 = x[..., :half].astype(jnp.float32)
    x2 = x[..., half:].astype(jnp.float32)
    return jnp.concatenate([x1 * cos - x2 * sin, x2 * cos + x1 * sin], -1).astype(x.dtype)

def in_projection(x, w_in, pos):
    bsz, n = x.shape[:2]
    z = x @ w_in
    cuts = [ATTN_DIM, ATTN_DIM + KV_DIM, ATTN_DIM + 2 * KV_DIM,
            ATTN_DIM + 2 * KV_DIM + CONV_DIM, ATTN_DIM + 2 * KV_DIM + 2 * CONV_DIM]
    q, k, v, gate_b, gate_c, h = jnp.split(z, cuts, axis=-1)
    q = rope(q.reshape(bsz, n, N_Q_HEADS, HEAD_DIM), pos)
    k = rope(k.reshape(bsz, n, N_KV_HEADS, HEAD_DIM), pos)
    v = v.reshape(bsz, n, N_KV_HEADS, HEAD_DIM)
    return q, k, v, gate_b, gate_c * h

def sink_attention(q, k, v, mask, sinks):
    bsz, nb, nq = q.shape[:3]
    qg = q.reshape(bsz, nb, nq, N_KV_HEADS, Q_PER_KV, HEAD_DIM)
    s = jnp.einsum('bnqkgd,bnskd->bnkgqs', qg, k,
                   preferred_element_type=jnp.float32) * (HEAD_DIM ** -0.5)
    s = jnp.where(mask[None, :, None, None], s, -jnp.inf)
    sink = sinks.astype(jnp.float32).reshape(1, 1, N_KV_HEADS, Q_PER_KV, 1, 1)
    m = jnp.maximum(s.max(-1, keepdims=True), sink)
    p = jnp.exp(s - m)
    p = p / (p.sum(-1, keepdims=True) + jnp.exp(sink - m))
    o = jnp.einsum('bnkgqs,bnskd->bnqkgd', p.astype(v.dtype), v)
    return o.reshape(bsz, nb * nq, ATTN_DIM)

def window_attention_prompt(q, k, v, sinks):
    bsz, n = q.shape[:2]
    nb = n // ATTN_BLOCK
    qb = q.reshape(bsz, nb, ATTN_BLOCK, N_Q_HEADS, HEAD_DIM)

    def band(t):
        tb = t.reshape(bsz, nb, ATTN_BLOCK, N_KV_HEADS, HEAD_DIM)
        prev = jnp.pad(tb[:, :-1], ((0, 0), (1, 0), (0, 0), (0, 0), (0, 0)))
        return jnp.concatenate([prev, tb], axis=2)

    blk = jnp.arange(nb)[:, None, None]
    qpos = blk * ATTN_BLOCK + jnp.arange(ATTN_BLOCK)[None, :, None]
    kpos = (blk - 1) * ATTN_BLOCK + jnp.arange(2 * ATTN_BLOCK)[None, None, :]
    d = qpos - kpos
    mask = (kpos >= 0) & (d >= 0) & (d <= WINDOW)
    return sink_attention(qb, band(k), band(v), mask, sinks)

def causal_conv(u_ext, w):
    n = u_ext.shape[1] - (CONV_K - 1)
    return sum(u_ext[:, j:j + n] * w[j] for j in range(CONV_K))

def mixer_prompt(x, w_in, w_o, sinks, conv_w):
    n = x.shape[1]
    pos = jnp.arange(n)
    q, k, v, gate_b, u = in_projection(x, w_in, pos)
    a = window_attention_prompt(q, k, v, sinks)
    c = causal_conv(jnp.pad(u, ((0, 0), (CONV_K - 1, 0), (0, 0))), conv_w)
    mix = jnp.concatenate([a, gate_b * c], -1) @ w_o
    buf = min(WINDOW, n)
    return mix, k[:, -buf:], v[:, -buf:], u[:, -(CONV_K - 1):]

def mixer_sample(x, k_cache, v_cache, conv_state, w_in, w_o, sinks, conv_w):
    n = x.shape[1]
    pos = PAST_LEN + jnp.arange(n)
    q, k, v, gate_b, u = in_projection(x, w_in, pos)
    buf = k_cache.shape[1]
    kk = jnp.concatenate([k_cache, k], 1)
    vv = jnp.concatenate([v_cache, v], 1)
    kpos = PAST_LEN - buf + jnp.arange(buf + n)
    d = pos[:, None] - kpos[None, :]
    mask = ((d >= 0) & (d <= WINDOW))[None]
    a = sink_attention(q[:, None], kk[:, None], vv[:, None], mask, sinks)
    u_ext = jnp.concatenate([conv_state, u], 1)
    c = causal_conv(u_ext, conv_w)
    mix = jnp.concatenate([a, gate_b * c], -1) @ w_o
    return mix, kk[:, -buf:], vv[:, -buf:], u_ext[:, -(CONV_K - 1):]

def hier_moe(x, w_rg, b_rg, w_re, b_re, w_gate, w_up, w_down):
    bsz, n, dm = x.shape
    x2 = x.reshape(bsz * n, dm)
    t = x2.shape[0]
    g_prob = jax.nn.softmax((x2 @ w_rg + b_rg).astype(jnp.float32), -1)
    grp = jnp.argmax(g_prob, -1)
    p_grp = jnp.take_along_axis(g_prob, grp[:, None], -1)
    e_logits = (x2 @ w_re + b_re).astype(jnp.float32).reshape(t, N_GROUPS, EXPERTS_PER_GROUP)
    e_logits = jnp.take_along_axis(e_logits, grp[:, None, None], 1)[:, 0]
    top_p, top_i = lax.top_k(jax.nn.softmax(e_logits, -1), TOP_K)
    gate = p_grp * top_p / top_p.sum(-1, keepdims=True)
    expert = grp[:, None] * EXPERTS_PER_GROUP + top_i
    a_n = t * TOP_K
    flat_e = expert.reshape(a_n)
    flat_tok = jnp.arange(a_n) // TOP_K
    order = jnp.argsort(flat_e)
    se = flat_e[order]
    counts = jnp.bincount(flat_e, length=N_EXPERTS)
    blk = max(8, min(MOE_BLOCK, a_n // N_EXPERTS))
    n_blocks = -(-a_n // blk) + N_EXPERTS
    padded = (counts + blk - 1) // blk * blk
    pad_end = jnp.cumsum(padded)
    pad_start = pad_end - padded
    start = jnp.cumsum(counts) - counts
    dest = pad_start[se] + jnp.arange(a_n) - start[se]
    xs = jnp.zeros((n_blocks * blk, dm), x2.dtype).at[dest].set(x2[flat_tok[order]])
    block_e = jnp.minimum(jnp.searchsorted(pad_end, jnp.arange(n_blocks) * blk, side='right'),
                          N_EXPERTS - 1)

    def expert_mlp(args):
        xb, e = args
        h = jax.nn.silu(xb @ w_gate[e]) * (xb @ w_up[e])
        return h @ w_down[e]

    ys = lax.map(expert_mlp, (xs.reshape(n_blocks, blk, dm), block_e)).reshape(n_blocks * blk, dm)
    y_sorted = ys[dest] * gate.reshape(a_n)[order][:, None].astype(x2.dtype)
    y = jnp.zeros((t, dm), x2.dtype).at[flat_tok[order]].add(y_sorted)
    return y.reshape(bsz, n, dm)

def setup_inputs(seed: int = 0) -> dict:
    key = jax.random.key(seed)
    ks = jax.random.split(key, 20)

    def nrm(k, shape, scale):
        return jax.random.normal(k, shape, jnp.float32) * scale

    buf = min(WINDOW, PAST_LEN)
    return {
        'x_prompt': nrm(ks[0], (BATCH, SEQ, D_MODEL), 1.0),
        'x_sample': nrm(ks[1], (DEC_BATCH, DEC_SEQ, D_MODEL), 1.0),
        'cache_k_win': nrm(ks[2], (DEPTH, DEC_BATCH, buf, N_KV_HEADS, HEAD_DIM), 1.0),
        'cache_v_win': nrm(ks[3], (DEPTH, DEC_BATCH, buf, N_KV_HEADS, HEAD_DIM), 1.0),
        'state_conv': nrm(ks[4], (DEPTH, DEC_BATCH, CONV_K - 1, CONV_DIM), 1.0),
        'w_in': nrm(ks[5], (DEPTH, D_MODEL, IN_DIM), D_MODEL ** -0.5),
        'w_o': nrm(ks[6], (DEPTH, MIX_DIM, D_MODEL), MIX_DIM ** -0.5 * DEEPNORM_BETA),
        'attn_sinks': nrm(ks[7], (DEPTH, N_Q_HEADS), 0.5),
        'conv_w': nrm(ks[8], (DEPTH, CONV_K, CONV_DIM), CONV_K ** -0.5),
        'ln1_g': 1.0 + nrm(ks[9], (DEPTH, D_MODEL), 0.02),
        'ln1_b': nrm(ks[10], (DEPTH, D_MODEL), 0.02),
        'w_router_group': nrm(ks[11], (DEPTH, D_MODEL, N_GROUPS), D_MODEL ** -0.5),
        'b_router_group': nrm(ks[12], (DEPTH, N_GROUPS), 0.01),
        'w_router_expert': nrm(ks[13], (DEPTH, D_MODEL, N_EXPERTS), D_MODEL ** -0.5),
        'b_router_expert': nrm(ks[14], (DEPTH, N_EXPERTS), 0.01),
        'w_gate': nrm(ks[15], (DEPTH, N_EXPERTS, D_MODEL, D_EXPERT), D_MODEL ** -0.5),
        'w_up': nrm(ks[16], (DEPTH, N_EXPERTS, D_MODEL, D_EXPERT), D_MODEL ** -0.5),
        'w_down': nrm(ks[17], (DEPTH, N_EXPERTS, D_EXPERT, D_MODEL), D_EXPERT ** -0.5 * DEEPNORM_BETA),
        'ln2_g': 1.0 + nrm(ks[18], (DEPTH, D_MODEL), 0.02),
        'ln2_b': nrm(ks[19], (DEPTH, D_MODEL), 0.02),
    }

def reference(x_prompt, x_sample, cache_k_win, cache_v_win, state_conv,
              w_in, w_o, attn_sinks, conv_w, ln1_g, ln1_b,
              w_router_group, b_router_group, w_router_expert, b_router_expert,
              w_gate, w_up, w_down, ln2_g, ln2_b):
    xp, xs = x_prompt, x_sample
    kp, vp, cp, ks_, vs_, cs_ = [], [], [], [], [], []
    for l in range(DEPTH):
        moe_w = (w_router_group[l], b_router_group[l], w_router_expert[l], b_router_expert[l],
                 w_gate[l], w_up[l], w_down[l])
        mix, k_buf, v_buf, c_buf = mixer_prompt(xp, w_in[l], w_o[l], attn_sinks[l], conv_w[l])
        xp = layer_norm(DEEPNORM_ALPHA * xp + mix, ln1_g[l], ln1_b[l])
        xp = layer_norm(DEEPNORM_ALPHA * xp + hier_moe(xp, *moe_w), ln2_g[l], ln2_b[l])
        kp.append(k_buf)
        vp.append(v_buf)
        cp.append(c_buf)
        mix, k_buf, v_buf, c_buf = mixer_sample(xs, cache_k_win[l], cache_v_win[l], state_conv[l],
                                                w_in[l], w_o[l], attn_sinks[l], conv_w[l])
        xs = layer_norm(DEEPNORM_ALPHA * xs + mix, ln1_g[l], ln1_b[l])
        xs = layer_norm(DEEPNORM_ALPHA * xs + hier_moe(xs, *moe_w), ln2_g[l], ln2_b[l])
        ks_.append(k_buf)
        vs_.append(v_buf)
        cs_.append(c_buf)
    return (xp, xs, jnp.stack(kp), jnp.stack(vp), jnp.stack(cp),
            jnp.stack(ks_), jnp.stack(vs_), jnp.stack(cs_))


_drawn_inputs = setup_inputs


def setup_inputs(seed=0):
    import zlib

    import numpy as np

    out = dict(_drawn_inputs(seed))
    spreads = {}
    factors = {'attn_sinks': 42.527, 'b_router_expert': 16.948, 'b_router_group': 8.0}
    for name, (base, spread) in spreads.items():
        noise = np.random.default_rng([zlib.crc32(name.encode()), seed]).standard_normal(out[name].shape)
        drawn = base * np.exp(spread * noise) if base else spread * noise
        out[name] = __import__('jax').numpy.asarray(drawn.astype(out[name].dtype))
    for name, factor in factors.items():
        out[name] = (out[name] * factor).astype(out[name].dtype)
    return out
```

```python
from contextlib import ExitStack, contextmanager

import numpy as np

import concourse.bass as bass
from concourse import mybir

F32 = mybir.dt.float32
I32 = mybir.dt.int32
ALU = mybir.AluOpType
ACT = mybir.ActivationFunctionType
AX = mybir.AxisListType

P = 128
DM = 1024
KD = DM // P
DEPTH = 2
SEQ = 1024
NS = 8
T = SEQ + NS
NB = SEQ // P
NT = NB + 1
HD, NH, NKV = 64, 8, 2
QPK = NH // NKV
NG, NE_G = 4, 8
NE = NG * NE_G
DE = 512
FD = DE // P
NR = NG + NE
CG = 4
NTILE = 6 + 3 * CG
CH = T // 3
NCH = 3
OVER = (2 * T) // P
NBLK = NE + OVER
ALPHA = (2 * DEPTH) ** 0.25
EPS = 1e-5
STEPS_LAYER = 321
STEPS_POOL = 147
BIG = 1e30
BASE = 1
BY_POOL = ("xg_in0", "xg_in1", "sc_out0", "sc_out1", "ov_x", "ov_sc")
SKIP = 1 << 20
PAST = 4096


def settle(eng, passed):
    eng.sem_inc(passed, 1)


class Steps:

    def __init__(self, eng, sem, passed=None):
        self.eng, self.sem, self.base, self.n, self.passed = eng, sem, 0, 0, passed

    def mark(self, ins):
        ins.then_inc(self.sem, 1)
        self.n += 1

    def wait(self):
        self.eng.wait_ge(self.sem, self.base + self.n)
        if self.passed is not None:
            settle(self.eng, self.passed)

    def link(self, ins):
        self.mark(ins)
        self.wait()

    @contextmanager
    def loop(self, count, per):
        base, n = self.base, self.n
        if self.passed is not None:
            settle(self.eng, self.passed)
        with self.eng.Fori(0, count) as i:
            self.base, self.n = base + n + i * per, 0
            yield i
            assert self.n == per, self.n
        self.base, self.n = base, n + count * per


def build(nc, a):
    ctx = ExitStack()
    with ctx:
        def sb(name, shape, dt=F32):
            return ctx.enter_context(nc.sbuf_tensor(name, shape, dt))

        def sem(name):
            return ctx.enter_context(nc.semaphore(name))

        def ds(i, n):
            return bass.ds(i, n)

        ident = sb("ident", [P, P])
        rotm = sb("rotm", [P, P])
        ones = sb("ones", [P, P])
        upper = sb("upper", [P, P])
        iota = sb("iota", [P, P])
        masks = sb("masks", [P, 3, 2 * P])
        cosT = sb("cosT", [P, T])
        sinT = sb("sinT", [P, T])
        rank_desc = sb("rank_desc", [P, NE])
        tokens1 = sb("tokens1", [P, 2 * NT])
        kscale = sb("kscale", [P, 2 * NT])
        valid = sb("valid", [P, NT])
        sel8 = sb("sel8", [64, NS])
        half_mask = sb("half_mask", [64, 2])
        sinks = sb("sinks", [P, DEPTH * NH])
        sinkc = sb("sinkc", [64, DEPTH])
        convw = sb("convw", [P, DEPTH, CG, 3])
        wr = sb("wr", [P, DEPTH, KD, NR])
        br = sb("br", [P, DEPTH, NR])
        lnp = sb("lnp", [P, 4, DM])
        mhalf = sb("mhalf", [P, 1])
        kwin = sb("kwin", [P, 2 * P])
        vnat = sb("vnat", [P, 2, P])
        logits = sb("logits", [P, NT, NR])
        inv = sb("inv", [P, 3, NBLK])
        gidx = sb("gidx", [P, NBLK], I32)
        sidx = sb("sidx", [P, NBLK], I32)
        gcol = sb("gcol", [P, 2], I32)
        scol = sb("scol", [P, 2], I32)
        rki = sb("rki", [P, 2 * NT + NE], I32)
        over_cmp = sb("over_cmp", [1, OVER, NE])
        over_f = sb("over_f", [1, OVER + 3])
        over = sb("over", [1, OVER + 3], I32)
        stat = sb("stat", [P, 12])
        mv = sb("mv", [P, 2, 2])
        rstd = sb("rstd", [P, 2, 2])
        sm = sb("sm", [P, 2, 5, QPK])
        rl = sb("rl", [P, NH])
        smp = sb("smp", [64, 8])
        su = sb("su", [P, CG * NS, 3])
        st = sb("st", [P, CG * NS, 2])
        upo = sb("upo", [P, CG, 2])
        arena = sb("arena", [P, 39040])

        def at(off, *shape, parts=P):
            n = int(np.prod(shape))
            v = arena[0:parts, off:off + n]
            if len(shape) == 2:
                return v.rearrange("p (a b) -> p a b", a=shape[0])
            if len(shape) == 4:
                return v.rearrange("p (a b c d) -> p a b c d", a=shape[0], b=shape[1], c=shape[2])
            if len(shape) == 3:
                return v.rearrange("p (a b c) -> p a b c", a=shape[0], b=shape[1])
            return v

        xT = at(0, KD, T)
        wo = at(0, KD, DM)
        zT = at(8256, 6, T)
        gT = at(14448, CG, T)
        wring = at(18576, 3, DM)
        ztmp = at(21648, 2, T)
        rot = at(23712, 2, CH)
        cbuf, hbuf, bbuf = at(24400, T), at(25432, T), at(26464, T)
        u = at(27496, SEQ + 2)
        acc = at(28528, SEQ)
        qs = at(18576, 2, 4, P)
        vs = at(19856, P)
        sS = at(20240, 2, QPK, 2 * P)
        pT = at(22288, 2, QPK, 2, P)
        oS = at(24336, NH * HD)
        mixT = at(24848, 2, KD, P)
        xres = at(26896, 2, DM)
        t1 = at(28944, DM)
        x1 = at(29968, 2, DM)
        x1T = at(32016, KD, P)
        kTs = at(33040, NS, P + 1)
        vS = at(34072, NS, P)
        qz = at(35096, NS * 72)
        ptz = at(35672, NS * 72)
        ss = at(36248, P + 1, parts=64)
        ssn = at(36384, P + 1, parts=64)
        diag = at(36520, 64, parts=64)
        pnew = at(36584, 64, parts=NS)
        vnew = at(36648, P, parts=NS)
        osel = at(36776, 64, parts=64)
        rt = [at(33040 + 288 * n, NT, NE) for n in range(10)]
        slot_of = at(35920, 2, P)
        block_of = at(36176, 2, 3 * NBLK)
        rk = at(36464, 12, 2 * NT)
        ovs = at(36680, 4, NE)
        wg, wu = at(0, 2, KD, DE), at(8192, 2, KD, DE)
        wd = at(16384, 2, FD, DM)
        xg = at(24576, 2, DM)
        xgT = at(26624, 2, KD, P)
        sg = at(28672, FD, P)
        hT = at(29184, 2, FD, P)
        ys = at(30208, 2, DM)
        l2in = at(8256, 2, 3 * DM)
        t2 = at(14400, 2, DM)
        x2 = at(16448, 2, DM)

        ps = ctx.enter_context(nc.psum_tensor("ps", [P, 8, 512], F32))

        s = {n: sem(n) for n in (
            "const_in", "init", "copied", "xin0", "xin1", "xt_mm", "xt_a", "xt_d", "x2_ready", "x2_out0",
            "x2_out1", "w_in0", "w_in1", "w_in2", "proj_mm", "act_ev", "rot_mm", "rot_used",
            "cos_done", "rope_done", "conv_done", "state_in", "state_set", "stage_done", "gate_staged", "v_t", "v_ev",
            "s_mm", "sm_ready", "p_ready", "pt_mm", "pt_ev", "pv_mm", "o_norm", "ot_mm", "ot_ev", "wo_in",
            "wo_mm", "xr_in0", "xr_in1", "ln_stat", "ln_rstd", "ln_hat", "ln_scaled", "ln_add", "x1_ready",
            "x1_out0", "x1_out1", "x1t_mm", "x1t_a", "x1t_d", "rt_mm", "lg_ev", "lnp_in", "smp_in",
            "smp_q", "smp_s", "smp_max", "smp_p", "smp_n", "smp_t", "smp_pt", "smp_o", "smp_sel", "smp_ot", "smp_mix",
            "small_out", "rk_m", "rk_c", "rk_r", "rk_inv", "idx_ready",
            "wg_in0", "wg_in1", "wu_in0", "wu_in1", "wd_in0", "wd_in1", "xg_in0", "xg_in1", "xg_mm",
            "xg_a", "xg_d", "gu_mm", "silu", "h_ready", "dn_mm", "y_a", "y_d", "sc_out0", "sc_out1",
            "l2_in0", "l2_in1", "l2_add", "l2_stat", "l2_rstd", "l2_hat", "l2_scaled", "dve_step", "pool_step",
            "pe_passed", "dve_passed", "pool_passed", "sp_passed", "rk_exp", "rk_soft",
            "ys_free", "ov_xin", "ov_out", "ov_w", "ov_x", "ov_col", "ov_xt", "ov_xa", "ov_gu", "ov_silu", "ov_h", "ov_dn", "ov_y", "ov_sc")}

        N_CONST = 21
        block = ctx.enter_context(nc.Block())

        SIGNALS = {
            "sync": (
                "const_in", "l2_in0", "l2_in1", "lnp_in", "ov_w", "small_out", "smp_in", "state_in", "w_in0",
                "w_in1", "w_in2", "wd_in0", "wd_in1", "wg_in0", "wg_in1", "wo_in", "wu_in0", "wu_in1", "x1_out0",
                "x1_out1", "x2_out0", "x2_out1", "xin0", "xin1", "xr_in0", "xr_in1"),
            "tensor": (
                "dn_mm", "gu_mm", "ot_mm", "ov_dn", "ov_gu", "ov_xt", "proj_mm", "pt_mm", "pv_mm", "rk_c", "rk_inv",
                "rot_mm", "rt_mm", "s_mm", "smp_o", "smp_ot", "smp_s", "smp_t", "v_t", "wo_mm", "x1t_mm", "xg_mm",
                "xt_mm"),
            "scalar": (
                "act_ev", "l2_hat", "ln_hat", "ot_ev", "ov_silu", "ov_xa", "p_ready", "pt_ev", "rk_exp", "silu",
                "smp_n", "x1t_a", "xg_a", "xt_a", "y_a"),
            "vector": (
                "conv_done", "h_ready", "idx_ready", "init", "l2_add", "l2_scaled", "l2_stat", "lg_ev", "ln_add",
                "ln_scaled", "ln_stat", "o_norm", "ov_h", "ov_y", "rk_m", "rk_r", "rk_soft", "rope_done",
                "rot_used", "sm_ready", "smp_max", "smp_mix", "smp_p", "smp_pt", "smp_sel", "v_ev", "x1t_d", "xg_d",
                "xt_d", "y_d"),
            "gpsimd": (
                "cos_done", "gate_staged", "l2_rstd", "ln_rstd", "ov_col", "ov_out", "ov_xin", "smp_q",
                "stage_done", "state_set", "x1_ready", "x2_ready", "ys_free"),
        }

        def raise_to_base(eng, name):
            for n in SIGNALS[name]:
                eng.sem_inc(s[n], BASE)

        @block.sync
        def _(sp):
            raise_to_base(sp, "sync")
            consts = [
                (ident, a["c_ident"]), (rotm, a["c_rot"]), (upper, a["c_upper"]), (iota, a["c_iota"]),
                (masks, a["c_masks"]), (cosT, a["c_cos"]), (sinT, a["c_sin"]), (rank_desc, a["c_desc"]),
                (tokens1, a["c_tok1"]), (kscale, a["c_k"]), (valid, a["c_valid"]), (sel8, a["c_sel8"]),
                (half_mask, a["c_half"]),
                (sinks, a["sinks"].partition_broadcast(P)), (sinkc, a["sinkc"]), (convw, a["conv_w"]),
            ]
            for l in range(DEPTH):
                consts.append((wr[:, l], a["w_r"][l].rearrange("(k p) n -> p k n", p=P)))
                consts.append((br[:, l], a["b_r"][l].partition_broadcast(P)))
            assert len(consts) + 1 == N_CONST, len(consts)
            for dst, src in consts:
                sp.dma_start(dst if isinstance(dst, bass.AP) else dst[:], src).then_inc(s["const_in"], 16)
            sp.dma_start(a["y_all"][0], a["x_all"]).then_inc(s["const_in"], 16)

            def x_tile(t, slot, rows):
                sp.dma_start(x2[0:rows, slot], a["x_all"][ds(t * P, rows), :]).then_inc(s[f"xin{slot}"], 16)

            x_tile(0, 0, P)
            x_tile(1, 1, P)
            settle(sp, s["sp_passed"])
            with sp.Fori(0, 3) as i:
                for slot in range(2):
                    sp.wait_ge(s["xt_mm"], BASE + 2 * i + slot + 3)
                    x_tile(2 * i + slot + 2, slot, P)
            sp.wait_ge(s["xt_mm"], BASE + 7 + 2)
            x_tile(8, 0, NS)

            with sp.Fori(0, DEPTH) as l:
                sp.wait_ge(s["x2_ready"], BASE + 9 * l)
                sp.wait_ge(s["x1_ready"], BASE + 9 * l)
                settle(sp, s["sp_passed"])
                sp.dma_start(lnp[:].rearrange("p a d -> p (a d)"), a["ln"][l].partition_broadcast(P)
                             ).then_inc(s["lnp_in"], 16)
                sp.wait_ge(s["small_out"], BASE + 16 * 7 * l)
                settle(sp, s["sp_passed"])
                sp.dma_start(st[:], a["state"][l]).then_inc(s["state_in"], 16)
                sp.dma_start(kTs[:, :, 0:P], a["cache_kT"][l]).then_inc(s["smp_in"], 16)
                sp.dma_start(vS, a["cache_v"][l].rearrange("b s d -> s b d")).then_inc(s["smp_in"], 16)

                def w_tile(c, slot):
                    sp.wait_ge(s["proj_mm"], BASE + (l * NTILE + c) * NCH)
                    settle(sp, s["sp_passed"])
                    sp.dma_start(wring[:, slot], a["w_in"][l, c]).then_inc(s[f"w_in{slot}"], 16)

                settle(sp, s["sp_passed"])
                with sp.Fori(0, NTILE // 3) as i:
                    for slot in range(3):
                        w_tile(3 * i + slot, slot)
                sp.wait_ge(s["proj_mm"], BASE + (l + 1) * NTILE * NCH + 6)
                settle(sp, s["sp_passed"])
                sp.dma_start(wo, a["w_o"][l].rearrange("(k p) n -> p k n", p=P)).then_inc(s["wo_in"], 16)

                def res_in(b, slot, rows, after):
                    sp.wait_ge(s["ln_add"], BASE + after)
                    settle(sp, s["sp_passed"])
                    sp.dma_start(xres[0:rows, slot], a["y_all"][l, ds(b * P, rows), :]
                                 ).then_inc(s[f"xr_in{slot}"], 16)

                def x1_out(b, slot, rows):
                    sp.wait_ge(s["x1_ready"], BASE + NT * l + b + 1)
                    settle(sp, s["sp_passed"])
                    sp.dma_start(a["xs1"][ds(b * P, rows), :], x1[0:rows, slot]).then_inc(s[f"x1_out{slot}"], 16)

                sp.wait_ge(s["conv_done"], BASE + (l + 1) * CG)
                sp.wait_ge(s["stage_done"], BASE + NB * l + 1)
                res_in(0, 0, P, NT * l)
                res_in(1, 1, P, NT * l)
                settle(sp, s["sp_passed"])
                with sp.Fori(0, 3) as i:
                    for slot in range(2):
                        res_in(2 * i + slot + 2, slot, P, NT * l + 2 * i + slot + 1)
                        x1_out(2 * i + slot, slot, P)
                res_in(8, 0, NS, NT * l + 7)
                x1_out(6, 0, P)
                x1_out(7, 1, P)
                x1_out(8, 0, NS)
                sp.wait_ge(s["smp_mix"], BASE + l + 1)
                settle(sp, s["sp_passed"])
                sp.wait_ge(s["stage_done"], BASE + NB * (l + 1))
                settle(sp, s["sp_passed"])
                sp.dma_start(a["o_kp"][l], zT[:, 0, SEQ - P:SEQ]).then_inc(s["small_out"], 16)
                sp.dma_start(a["o_vp"][l], zT[:, 5, SEQ - P:SEQ]).then_inc(s["small_out"], 16)
                sp.dma_start(a["o_ks"][l], kTs[:, :, 1:P + 1]).then_inc(s["small_out"], 16)
                sp.dma_start(a["o_vs"][l, :, 0:P - 1, :].rearrange("b s d -> s b d"), vS[1:P]
                             ).then_inc(s["small_out"], 16)
                sp.dma_start(a["o_vs"][l, :, P - 1, :], vnew).then_inc(s["small_out"], 16)
                sp.dma_start(a["o_cp"][l], upo[:]).then_inc(s["small_out"], 16)
                sp.dma_start(a["o_cs"][l], su[:]).then_inc(s["small_out"], 16)

                def expert_in(e, slot):
                    sp.wait_ge(s["gu_mm"], BASE + 2 * (NE * l + e) + 2)
                    settle(sp, s["sp_passed"])
                    sp.dma_start(wg[:, slot], a["w_gate"][l, e].rearrange("(k p) f -> p k f", p=P)
                                 ).then_inc(s[f"wg_in{slot}"], 16)
                    sp.dma_start(wu[:, slot], a["w_up"][l, e].rearrange("(k p) f -> p k f", p=P)
                                 ).then_inc(s[f"wu_in{slot}"], 16)
                    sp.wait_ge(s["dn_mm"], BASE + NE * l + e + 1)
                    settle(sp, s["sp_passed"])
                    sp.dma_start(wd[:, slot], a["w_down"][l, e].rearrange("(k p) f -> p k f", p=P)
                                 ).then_inc(s[f"wd_in{slot}"], 16)

                sp.wait_ge(s["small_out"], BASE + 16 * 7 * (l + 1))
                settle(sp, s["sp_passed"])
                sp.wait_ge(s["rt_mm"], BASE + NT * (l + 1))
                settle(sp, s["sp_passed"])
                sp.wait_ge(s["x1_out0"], BASE + 16 * 5 * (l + 1))
                settle(sp, s["sp_passed"])
                sp.wait_ge(s["x1_out1"], BASE + 16 * 4 * (l + 1))
                settle(sp, s["sp_passed"])
                with sp.Fori(0, NE // 2) as i:
                    for slot in range(2):
                        expert_in(2 * i + slot, slot)

                sp.wait_ge(s["idx_ready"], BASE + l + 1)
                settle(sp, s["sp_passed"])
                with sp.If(sp.value_load(over[0:1, OVER:OVER + 1], min_val=0, max_val=OVER) > 0):
                    sp.wait_ge(s["dn_mm"], BASE + NE * (l + 1) + 2)
                    settle(sp, s["sp_passed"])
                    with sp.Fori(0, OVER) as o:
                        sp.wait_ge(s["ov_dn"], BASE + OVER * l + o)
                        settle(sp, s["sp_passed"])
                        e = sp.value_load(over[0:1, ds(o, 1)], min_val=0, max_val=NE - 1)
                        for dst, w in ((wg[:, 0], "w_gate"), (wu[:, 0], "w_up"), (wd[:, 0], "w_down")):
                            sp.dma_start(dst, a[w][l, e].rearrange("(k p) f -> p k f", p=P)
                                         ).then_inc(s["ov_w"], 16)
                with sp.Else():
                    sp.sem_inc(s["ov_w"], 48 * OVER)
                sp.wait_ge(s["ov_out"], BASE + OVER * (l + 1))
                settle(sp, s["sp_passed"])

                def l2(t, slot, rows, after):
                    sp.wait_ge(s["l2_add"], BASE + after)
                    settle(sp, s["sp_passed"])
                    for n, src in enumerate((a["ytok"][0], a["ytok"][1], a["xs1"])):
                        sp.dma_start(l2in[0:rows, slot, n * DM:(n + 1) * DM], src[ds(t * P, rows), :]
                                     ).then_inc(s[f"l2_in{slot}"], 16)

                def x2_out(t, slot, rows):
                    sp.wait_ge(s["x2_ready"], BASE + NT * l + t + 1)
                    settle(sp, s["sp_passed"])
                    sp.dma_start(a["y_all"][l + 1, ds(t * P, rows), :], x2[0:rows, slot]
                                 ).then_inc(s[f"x2_out{slot}"], 16)

                sp.wait_ge(s["sc_out0"], 16 * (NE // 2) * (l + 1))
                sp.wait_ge(s["sc_out1"], 16 * (NE // 2) * (l + 1))
                l2(0, 0, P, NT * l)
                l2(1, 1, P, NT * l)
                settle(sp, s["sp_passed"])
                with sp.Fori(0, 3) as i:
                    for slot in range(2):
                        l2(2 * i + slot + 2, slot, P, NT * l + 2 * i + slot + 1)
                        x2_out(2 * i + slot, slot, P)
                l2(8, 0, NS, NT * l + 7)
                x2_out(6, 0, P)
                x2_out(7, 1, P)
                x2_out(8, 0, NS)
                sp.wait_ge(s["x2_out0"], BASE + 16 * 5 * (l + 1))
                settle(sp, s["sp_passed"])
                sp.wait_ge(s["x2_out1"], BASE + 16 * 4 * (l + 1))
                settle(sp, s["sp_passed"])

        @block.tensor
        def _(pe):
            raise_to_base(pe, "tensor")
            mm = nc.tensor.matmul
            tr = nc.tensor.transpose
            pe.sem_inc(s["xt_mm"], 2)
            pe.sem_inc(s["proj_mm"], 6)
            pe.sem_inc(s["wo_mm"], 2)
            pe.sem_inc(s["gu_mm"], 4)
            pe.sem_inc(s["dn_mm"], 2)
            pe.sem_inc(s["xg_mm"], 2)
            pe.wait_ge(s["const_in"], BASE + 16 * N_CONST)
            pe.wait_ge(s["init"], BASE + 6)

            def x_transposed(g, slot, rows):
                pe.wait_ge(s["xt_a"], BASE + g + 1)
                pe.wait_ge(s["xt_d"], BASE + g + 1)
                if rows < P:
                    settle(pe, s["pe_passed"])
                for k in range(KD):
                    last = tr(ps[:, 2 * slot + k // 4, (k % 4) * P:(k % 4) * P + rows],
                              x2[0:rows, slot, k * P:(k + 1) * P], ident[0:rows, 0:rows])
                last.then_inc(s["xt_mm"], 1)

            settle(pe, s["pe_passed"])
            with pe.Fori(0, 4) as i:
                for slot in range(2):
                    pe.wait_ge(s[f"xin{slot}"], BASE + 16 * (i + 1))
                    x_transposed(2 * i + slot, slot, P)
            pe.wait_ge(s["xin0"], BASE + 16 * 5)
            x_transposed(8, 0, NS)

            with pe.Fori(0, DEPTH) as l:
                pe.wait_ge(s["xt_a"], BASE + NT * (l + 1) + 2)
                pe.wait_ge(s["xt_d"], BASE + NT * (l + 1) + 2)

                def project(c, slot, half, turn):
                    pe.wait_ge(s[f"w_in{slot}"], BASE + 16 * (6 * l + turn + 1))
                    for ch in range(NCH):
                        pe.wait_ge(s["act_ev"], BASE + (l * NTILE + c) * NCH + ch + 1)
                        for k in range(KD):
                            last = mm(ps[:, 3 * half + ch, 0:CH], wring[:, slot, k * P:(k + 1) * P],
                                      xT[:, k, ch * CH:(ch + 1) * CH], start=(k == 0), stop=(k == KD - 1))
                        last.then_inc(s["proj_mm"], 1)

                def rotate(r):
                    for ch in range(NCH):
                        i = NCH * r + ch
                        pe.wait_ge(s["act_ev"], BASE + (l * NTILE + r) * NCH + ch + 1 + 6)
                        pe.wait_ge(s["rot_used"], BASE + 15 * l + max(i - 1, 0))
                        mm(ps[:, 6 + i % 2, 0:CH], rotm[:], ztmp[:, r % 2, ch * CH:(ch + 1) * CH],
                           start=True, stop=True).then_inc(s["rot_mm"], 1)

                for c in range(6):
                    project(c, c % 3, c % 2, c // 3)
                    if c:
                        rotate(c - 1)
                settle(pe, s["pe_passed"])
                with pe.Fori(0, CG // 2) as i:
                    for n in range(6):
                        project(6 + 6 * i + n, n % 3, n % 2, 2 + 2 * i + n // 3)

                pe.wait_ge(s["wo_in"], BASE + 16 * (l + 1))
                pe.wait_ge(s["lnp_in"], BASE + 16 * (l + 1))

                def scores(b, slot):
                    n = NB * l + b
                    pe.wait_ge(s["stage_done"], BASE + n + 1)
                    pe.wait_ge(s["o_norm"], BASE + n)
                    tr(ps[:, 4, 0:P], vs, ident[:]).then_inc(s["v_t"], 1)
                    pe.wait_ge(s["pt_ev"], BASE + 2 * n)
                    for h in range(NKV):
                        for j in range(QPK):
                            last = mm(ps[:, 2 * h + j // 2, (j % 2) * 256:(j % 2) * 256 + 256],
                                      qs[h * HD:(h + 1) * HD, slot, j], kwin[h * HD:(h + 1) * HD, :],
                                      start=True, stop=True)
                        last.then_inc(s["s_mm"], 1)

                def weighted_values(b, slot):
                    n = NB * l + b
                    for h in range(NKV):
                        pe.wait_ge(s["p_ready"], BASE + 2 * n + h + 1)
                        for j in range(QPK):
                            for w in range(2):
                                last = tr(ps[:, 2 * h + j // 2, (j % 2) * 256 + w * P:(j % 2) * 256 + (w + 1) * P],
                                          sS[:, h, j, w * P:(w + 1) * P], ident[:])
                        last.then_inc(s["pt_mm"], 1)
                    pe.wait_ge(s["v_ev"], BASE + n + 1)
                    for h in range(NKV):
                        pe.wait_ge(s["pt_ev"], BASE + 2 * n + h + 1)
                        for j in range(QPK):
                            c = (QPK * h + j) * HD
                            for w in range(2):
                                last = mm(ps[:, 4, c:c + HD], pT[:, h, j, w], vnat[:, w, h * HD:(h + 1) * HD],
                                          start=(w == 0), stop=(w == 1))
                    last.then_inc(s["pv_mm"], 1)

                def o_transposed(b):
                    n = NB * l + b
                    pe.wait_ge(s["o_norm"], BASE + n + 1)
                    pe.wait_ge(s["lg_ev"], BASE + NT * l + b)
                    for j in range(4):
                        last = tr(ps[:, 5, j * P:(j + 1) * P], oS[:, j * P:(j + 1) * P], ident[:])
                    last.then_inc(s["ot_mm"], 1)

                def out_project(b, slot, rows):
                    m = NT * l + b
                    if rows == P:
                        pe.wait_ge(s["ot_ev"], BASE + NB * l + b + 1)
                    else:
                        pe.wait_ge(s["smp_mix"], BASE + l + 1)
                    pe.wait_ge(s["gate_staged"], BASE + m + 1)
                    pe.wait_ge(s["x1t_a"], BASE + m)
                    pe.wait_ge(s["x1t_d"], BASE + m)
                    for n in range(2):
                        for k in range(KD):
                            last = mm(ps[0:rows, 6 + n, :], mixT[:, slot, k, 0:rows], wo[:, k, n * 512:(n + 1) * 512],
                                      start=(k == 0), stop=(k == KD - 1))
                    last.then_inc(s["wo_mm"], 1)

                def route(b, slot, rows):
                    m = NT * l + b
                    pe.wait_ge(s["x1_ready"], BASE + m + 1)
                    if rows < P:
                        settle(pe, s["pe_passed"])
                    for k in range(KD):
                        last = tr(ps[:, 6 + k // 4, (k % 4) * P:(k % 4) * P + rows],
                                  x1[0:rows, slot, k * P:(k + 1) * P], ident[0:rows, 0:rows])
                    last.then_inc(s["x1t_mm"], 1)
                    pe.wait_ge(s["x1t_a"], BASE + m + 1)
                    pe.wait_ge(s["x1t_d"], BASE + m + 1)
                    settle(pe, s["pe_passed"])
                    for k in range(KD):
                        last = mm(ps[0:rows, 5, 0:NR], x1T[:, k, 0:rows], wr_l[k], start=(k == 0), stop=(k == KD - 1))
                    last.then_inc(s["rt_mm"], 1)

                wr_l = [wr[:, ds(l, 1), k, :].rearrange("p a n -> p (a n)") for k in range(KD)]
                scores(0, 0)
                weighted_values(0, 0)
                o_transposed(0)
                settle(pe, s["pe_passed"])
                with pe.Fori(0, 3) as i:
                    for n in range(2):
                        b, slot = 2 * i + n + 1, (n + 1) % 2
                        scores(b, slot)
                        out_project(b - 1, 1 - slot, P)
                        weighted_values(b, slot)
                        route(b - 1, 1 - slot, P)
                        o_transposed(b)
                scores(7, 1)
                out_project(6, 0, P)
                weighted_values(7, 1)
                route(6, 0, P)
                o_transposed(7)

                pe.wait_ge(s["smp_q"], BASE + l + 1)
                pe.wait_ge(s["smp_in"], BASE + 32 * (l + 1))
                pe.wait_ge(s["pt_ev"], BASE + 2 * NB * (l + 1))
                for b in range(NS):
                    last = mm(ps[0:64, 0, 0:P + 1], qz[:, b * 64:(b + 1) * 64], kTs[:, b, :],
                              start=(b == 0), stop=(b == NS - 1))
                last.then_inc(s["smp_s"], 1)
                out_project(7, 1, P)
                pe.wait_ge(s["smp_p"], BASE + l + 1)
                settle(pe, s["pe_passed"])
                tr(ps[:, 1, 0:64], ssn[:, 0:P], ident[0:64, 0:64])
                mm(ps[0:NS, 2, 0:64], sel8[:], diag, start=True, stop=True)
                tr(ps[0:NS, 3, 0:P], zT[:, 5, SEQ:T], ident[:]).then_inc(s["smp_t"], 1)
                pe.wait_ge(s["smp_pt"], BASE + l + 1)
                for b in range(NS):
                    mm(ps[0:64, 4, 0:P], ptz[:, b * 64:(b + 1) * 64], vS[:, b, :], start=(b == 0), stop=False)
                mm(ps[0:64, 4, 0:P], pnew, vnew, start=False, stop=True).then_inc(s["smp_o"], 1)
                pe.wait_ge(s["smp_sel"], BASE + l + 1)
                settle(pe, s["pe_passed"])
                tr(ps[0:64, 1, 0:64], osel, ident[0:64, 0:64]).then_inc(s["smp_ot"], 1)
                route(7, 1, P)
                out_project(8, 0, NS)
                route(8, 0, NS)

                pe.wait_ge(s["rk_m"], BASE + l + 1)
                for t in range(NT):
                    mm(ps[:, 4, t * NE:(t + 1) * NE], upper[:], rt[4][:, t, :], start=True, stop=False)
                    mm(ps[:, 4, t * NE:(t + 1) * NE], ones[:], rt[5][:, t, :], start=False, stop=True)
                mm(ps[:, 5, 0:NE], ones[:], rt[6][:, 0, :], start=True, stop=True).then_inc(s["rk_c"], 1)
                for i in range(2 * NT):
                    pe.wait_ge(s["rk_r"], BASE + 2 * NT * l + i + 1)
                    mm(ps[:, 0, 0:3 * NBLK], slot_of[:, i % 2], block_of[:, i % 2],
                       start=(i == 0), stop=(i == 2 * NT - 1)).then_inc(s["rk_inv"], 1)

                def gathered(e, slot, turn):
                    n = NE * l + e
                    pe.wait_ge(s[f"xg_in{slot}"], 16 * (NE // 2 * l + turn + 1))
                    pe.wait_ge(s["xg_a"], BASE + n)
                    pe.wait_ge(s["xg_d"], BASE + n)
                    for k in range(KD):
                        last = tr(ps[:, k // 4, (k % 4) * P:(k % 4 + 1) * P], xg[:, slot, k * P:(k + 1) * P], ident[:])
                    last.then_inc(s["xg_mm"], 1)

                def gate_up(e, slot, turn):
                    n = NE * l + e
                    pe.wait_ge(s["xg_a"], BASE + n + 1)
                    pe.wait_ge(s["xg_d"], BASE + n + 1)
                    pe.wait_ge(s[f"wg_in{slot}"], BASE + 16 * (NE // 2 * l + turn + 1))
                    pe.wait_ge(s[f"wu_in{slot}"], BASE + 16 * (NE // 2 * l + turn + 1))
                    pe.wait_ge(s["h_ready"], BASE + 2 * n + 2)
                    for f in range(FD):
                        bank, c = 2 + 2 * slot + f // 2, (f % 2) * P
                        for w, at_c in ((wg, c), (wu, c + 2 * P)):
                            for k in range(KD):
                                last = mm(ps[:, bank, at_c:at_c + P], w[:, slot, k, f * P:(f + 1) * P],
                                          xgT[:, slot, k], start=(k == 0), stop=(k == KD - 1))
                        if f % 2:
                            last.then_inc(s["gu_mm"], 1)

                def down(e, slot, turn):
                    n = NE * l + e
                    pe.wait_ge(s["h_ready"], BASE + 2 * n + 2 + 4)
                    pe.wait_ge(s[f"wd_in{slot}"], BASE + 16 * (NE // 2 * l + turn + 1))
                    pe.wait_ge(s["y_a"], BASE + n)
                    pe.wait_ge(s["y_d"], BASE + n)
                    for h in range(2):
                        for f in range(FD):
                            last = mm(ps[:, 6 + h, :], hT[:, slot, f], wd[:, slot, f, h * 512:(h + 1) * 512],
                                      start=(f == 0), stop=(f == FD - 1))
                    last.then_inc(s["dn_mm"], 1)

                gathered(0, 0, 0)
                settle(pe, s["pe_passed"])
                with pe.Fori(0, NE // 2 - 1) as i:
                    gate_up(2 * i, 0, i)
                    gathered(2 * i + 1, 1, i)
                    down(2 * i, 0, i)
                    gate_up(2 * i + 1, 1, i)
                    gathered(2 * i + 2, 0, i + 1)
                    down(2 * i + 1, 1, i)
                i = NE // 2 - 1
                gate_up(2 * i, 0, i)
                gathered(2 * i + 1, 1, i)
                down(2 * i, 0, i)
                gate_up(2 * i + 1, 1, i)
                down(2 * i + 1, 1, i)

                settle(pe, s["pe_passed"])
                with pe.If(pe.value_load(over[0:1, OVER:OVER + 1], min_val=0, max_val=OVER) > 0):
                    pe.wait_ge(s["y_a"], BASE + NE * (l + 1))
                    pe.wait_ge(s["y_d"], BASE + NE * (l + 1))
                    settle(pe, s["pe_passed"])
                    with pe.Fori(0, OVER) as o:
                        n = OVER * l + o
                        pe.wait_ge(s["ov_xin"], BASE + n + 1)
                        for k in range(KD):
                            last = tr(ps[:, k // 4, (k % 4) * P:(k % 4 + 1) * P], xg[:, 0, k * P:(k + 1) * P], ident[:])
                        last.then_inc(s["ov_xt"], 1)
                        pe.wait_ge(s["ov_xa"], BASE + n + 1)
                        pe.wait_ge(s["ov_w"], BASE + 48 * (n + 1))
                        for f in range(FD):
                            for w, bank in ((wg, 2), (wu, 4)):
                                for k in range(KD):
                                    last = mm(ps[:, bank, f * P:(f + 1) * P], w[:, 0, k, f * P:(f + 1) * P],
                                              xgT[:, 0, k], start=(k == 0), stop=(k == KD - 1))
                        last.then_inc(s["ov_gu"], 1)
                        pe.wait_ge(s["ov_h"], BASE + n + 1)
                        for h in range(2):
                            for f in range(FD):
                                last = mm(ps[:, 6 + h, :], hT[:, 0, f], wd[:, 0, f, h * 512:(h + 1) * 512],
                                          start=(f == 0), stop=(f == FD - 1))
                        last.then_inc(s["ov_dn"], 1)
                with pe.Else():
                    pe.sem_inc(s["ov_xt"], OVER)
                    pe.sem_inc(s["ov_gu"], OVER)
                    pe.sem_inc(s["ov_dn"], OVER)

                settle(pe, s["pe_passed"])
                with pe.Fori(0, 4) as i:
                    for slot in range(2):
                        pe.wait_ge(s["x2_ready"], BASE + NT * l + 2 * i + slot + 1)
                        x_transposed(NT * (l + 1) + 2 * i + slot, slot, P)
                pe.wait_ge(s["x2_ready"], BASE + NT * l + 9)
                x_transposed(NT * (l + 1) + 8, 0, NS)

        @block.scalar
        def _(act):
            raise_to_base(act, "scalar")
            act.sem_inc(s["xt_a"], 2)
            act.sem_inc(s["act_ev"], 6)

            def xt_evict(g, slot, col, rows):
                act.wait_ge(s["xt_mm"], BASE + g + 3)
                nc.scalar.copy(xT[:, 0:4, ds(col, rows)],
                               ps[:, 2 * slot, :].rearrange("p (k t) -> p k t", k=4)[:, :, 0:rows]
                               ).then_inc(s["xt_a"], 1)

            def xt_tiles(g0):
                with act.Fori(0, 4) as i:
                    for slot in range(2):
                        xt_evict(g0 + 2 * i + slot, slot, (2 * i + slot) * P, P)
                xt_evict(g0 + 8, 0, SEQ, NS)

            xt_tiles(0)

            with act.Fori(0, DEPTH) as l:
                def evict(c, half, dst, wait=None):
                    for ch in range(NCH):
                        n = (l * NTILE + c) * NCH + ch
                        act.wait_ge(s["proj_mm"], BASE + n + 1 + 6)
                        nc.scalar.copy(dst[:, ch * CH:(ch + 1) * CH], ps[:, 3 * half + ch, 0:CH]
                                       ).then_inc(s["act_ev"], 1)

                for c in range(5):
                    act.wait_ge(s["rot_mm"], BASE + 15 * l + max(c - 1, 0) * NCH)
                    act.wait_ge(s["cos_done"], BASE + 15 * l + max(c - 1, 0) * NCH)
                    evict(c, c % 2, ztmp[:, c % 2])
                evict(5, 1, zT[:, 5])
                with act.Fori(0, CG // 2) as i:
                    for n in range(6):
                        if n % 3 == 0:
                            act.wait_ge(s["conv_done"], BASE + CG * l + 2 * i + n // 3)
                        evict(6 + 6 * i + n, n % 2, (cbuf, hbuf, bbuf)[n % 3])

                def softmax(b):
                    n = NB * l + b
                    for h in range(NKV):
                        act.wait_ge(s["sm_ready"], BASE + 2 * n + h + 1)
                        for j in range(QPK):
                            nc.scalar.activation(sS[:, h, j], sS[:, h, j], ACT.Exp, bias=sm[:, h, 1, j:j + 1],
                                                 accum_out=sm[:, h, 3, j:j + 1])
                        nc.scalar.activation(sm[:, h, 4], sm[:, h, 2], ACT.Exp).then_inc(s["p_ready"], 1)

                def pt_evict(b):
                    n = NB * l + b
                    act.wait_ge(s["pv_mm"], BASE + n)
                    for h in range(NKV):
                        act.wait_ge(s["pt_mm"], BASE + 2 * n + h + 1)
                        nc.scalar.copy(pT[:, h].rearrange("p j w k -> p (j w k)"),
                                       ps[:, 2 * h:2 * h + 2, :].rearrange("p a b -> p (a b)")
                                       ).then_inc(s["pt_ev"], 1)

                def normed(b, rows):
                    m = NT * l + b
                    act.wait_ge(s["ln_rstd"], BASE + m + 1)
                    nc.scalar.activation(t1[0:rows], t1[0:rows], ACT.Identity, bias=rstd[0:rows, 0, 1:2],
                                         scale=rstd[0:rows, 0, 0:1]).then_inc(s["ln_hat"], 1)

                def x1t_evict(b, rows):
                    m = NT * l + b
                    act.wait_ge(s["x1t_mm"], BASE + m + 1)
                    act.wait_ge(s["rt_mm"], BASE + m)
                    nc.scalar.copy(x1T[:, 0:4, 0:rows],
                                   ps[:, 6, :].rearrange("p (k t) -> p k t", k=4)[:, :, 0:rows]
                                   ).then_inc(s["x1t_a"], 1)

                def ot_evict(b, slot):
                    act.wait_ge(s["ot_mm"], BASE + NB * l + b + 1)
                    act.wait_ge(s["wo_mm"], BASE + NT * l + b + 1)
                    nc.scalar.copy(mixT[:, slot, 0:4].rearrange("p k t -> p (k t)"), ps[:, 5, :]
                                   ).then_inc(s["ot_ev"], 1)

                softmax(0)
                pt_evict(0)
                ot_evict(0, 0)
                with act.Fori(0, 3) as i:
                    for n in range(2):
                        b, slot = 2 * i + n + 1, (n + 1) % 2
                        softmax(b)
                        pt_evict(b)
                        normed(b - 1, P)
                        x1t_evict(b - 1, P)
                        ot_evict(b, slot)
                softmax(7)
                pt_evict(7)
                normed(6, P)
                x1t_evict(6, P)
                ot_evict(7, 1)

                act.wait_ge(s["smp_max"], BASE + l + 1)
                nc.scalar.activation(ss, ss, ACT.Exp, bias=smp[:, 1:2], accum_out=smp[:, 3:4])
                nc.scalar.activation(smp[:, 4:5], smp[:, 2:3], ACT.Exp).then_inc(s["smp_n"], 1)
                normed(7, P)
                x1t_evict(7, P)
                normed(8, NS)
                x1t_evict(8, NS)

                act.wait_ge(s["rk_soft"], BASE + l + 1)
                nc.scalar.activation(rt[7][:, :, 0:NG], rt[7][:, :, 0:NG], ACT.Exp)
                nc.scalar.activation(rt[7][:, :, 8:9], rt[7][:, :, 8:9], ACT.Exp).then_inc(s["rk_exp"], 1)

                def xg_evict(e, slot):
                    n = NE * l + e
                    act.wait_ge(s["xg_mm"], BASE + n + 3)
                    act.wait_ge(s["gu_mm"], BASE + 2 * n + 2)
                    nc.scalar.copy(xgT[:, slot, 0:4].rearrange("p k t -> p (k t)"), ps[:, 0, :]
                                   ).then_inc(s["xg_a"], 1)

                def silu(e, slot):
                    n = NE * l + e
                    for q in range(2):
                        act.wait_ge(s["gu_mm"], BASE + 2 * n + q + 1 + 4)
                        act.wait_ge(s["h_ready"], BASE + 2 * n + q - 1 + 4)
                        nc.scalar.activation(sg[:, 2 * q:2 * q + 2].rearrange("p f t -> p (f t)"),
                                             ps[:, 2 + 2 * slot + q, 0:2 * P], ACT.Silu
                                             ).then_inc(s["silu"], 1)

                def y_evict(e, slot, turn, col):
                    n = NE * l + e
                    act.wait_ge(s["dn_mm"], BASE + n + 3)
                    act.wait_ge(s["ys_free"], BASE + n + 1)
                    nc.scalar.activation(ys[:, slot, 0:512], ps[:, 6, :], ACT.Copy, scale=col).then_inc(s["y_a"], 1)

                def gate_of(e):
                    return inv[:, 2, ds(e, 1)]

                xg_evict(0, 0)
                with act.Fori(0, NE // 2 - 1) as i:
                    silu(2 * i, 0)
                    xg_evict(2 * i + 1, 1)
                    y_evict(2 * i, 0, i, gate_of(2 * i))
                    silu(2 * i + 1, 1)
                    xg_evict(2 * i + 2, 0)
                    y_evict(2 * i + 1, 1, i, gate_of(2 * i + 1))
                i = NE // 2 - 1
                silu(2 * i, 0)
                xg_evict(2 * i + 1, 1)
                y_evict(2 * i, 0, i, gate_of(2 * i))
                silu(2 * i + 1, 1)
                y_evict(2 * i + 1, 1, i, gate_of(2 * i + 1))

                with act.If(act.value_load(over[0:1, OVER:OVER + 1], min_val=0, max_val=OVER) > 0):
                    with act.Fori(0, OVER) as o:
                        n = OVER * l + o
                        act.wait_ge(s["ov_xt"], BASE + n + 1)
                        nc.scalar.copy(xgT[:, 0].rearrange("p k t -> p (k t)"),
                                       ps[:, 0:2, :].rearrange("p a b -> p (a b)")).then_inc(s["ov_xa"], 1)
                        act.wait_ge(s["ov_gu"], BASE + n + 1)
                        nc.scalar.activation(sg.rearrange("p f t -> p (f t)"), ps[:, 2, :], ACT.Silu
                                             ).then_inc(s["ov_silu"], 1)
                with act.Else():
                    act.sem_inc(s["ov_xa"], OVER)
                    act.sem_inc(s["ov_silu"], OVER)

                def normed2(t, slot, rows):
                    act.wait_ge(s["l2_rstd"], BASE + NT * l + t + 1)
                    nc.scalar.activation(t2[0:rows, slot], t2[0:rows, slot], ACT.Identity,
                                         bias=rstd[0:rows, slot, 1:2], scale=rstd[0:rows, slot, 0:1]
                                         ).then_inc(s["l2_hat"], 1)

                normed2(0, 0, P)
                with act.Fori(0, 3) as i:
                    for n in range(2):
                        normed2(2 * i + n + 1, 1 - n, P)
                        xt_evict(NT * (l + 1) + 2 * i + n, n, (2 * i + n) * P, P)
                normed2(7, 1, P)
                xt_evict(NT * (l + 1) + 6, 0, 6 * P, P)
                normed2(8, 0, NS)
                xt_evict(NT * (l + 1) + 7, 1, 7 * P, P)
                xt_evict(NT * (l + 1) + 8, 0, SEQ, NS)

        @block.vector
        def _(dve):
            raise_to_base(dve, "vector")
            v = nc.vector
            step = Steps(dve, s["dve_step"])
            dve.sem_inc(s["xt_d"], 2)
            dve.sem_inc(s["h_ready"], 4)
            v.memset(ones[:], 1.0).then_inc(s["init"], 1)
            v.memset(mhalf[:], -0.5).then_inc(s["init"], 1)
            v.memset(kwin[:], 0.0).then_inc(s["init"], 1)
            v.memset(vnat[:], 0.0).then_inc(s["init"], 1)
            v.memset(logits[:], 0.0).then_inc(s["init"], 1)
            v.memset(over_f[:], 0.0).then_inc(s["init"], 1)
            dve.wait_ge(s["init"], BASE + 6)
            dve.wait_ge(s["const_in"], BASE + 16 * N_CONST)

            def xt_evict(g, slot, col, rows):
                dve.wait_ge(s["xt_mm"], BASE + g + 3)
                v.tensor_copy(xT[:, 4:8, ds(col, rows)],
                              ps[:, 2 * slot + 1, :].rearrange("p (k t) -> p k t", k=4)[:, :, 0:rows]
                              ).then_inc(s["xt_d"], 1)

            settle(dve, s["dve_passed"])
            with dve.Fori(0, 4) as i:
                for slot in range(2):
                    xt_evict(2 * i + slot, slot, (2 * i + slot) * P, P)
            xt_evict(8, 0, SEQ, NS)

            def moments(t, slot, rows, done):
                for h in range(2):
                    step.mark(v.bn_stats(stat[0:rows, 6 * h:6 * h + 6], t[:, h * 512:(h + 1) * 512]))
                step.wait()
                settle(dve, s["dve_passed"])
                v.bn_aggr(mv[0:rows, slot], stat[0:rows]).then_inc(done, 1)

            with step.loop(DEPTH, STEPS_LAYER) as l:
                for r in range(5):
                    for ch in range(NCH):
                        i = NCH * r + ch
                        cols = slice(ch * CH, (ch + 1) * CH)
                        dve.wait_ge(s["rot_mm"], BASE + 15 * l + i + 1)
                        v.tensor_tensor(rot[:, i % 2], ps[:, 6 + i % 2, 0:CH], sinT[:, cols], ALU.mult
                                        ).then_inc(s["rot_used"], 1)
                        dve.wait_ge(s["rot_used"], BASE + 15 * l + i + 1)
                        dve.wait_ge(s["cos_done"], BASE + 15 * l + i + 1)
                        v.tensor_tensor(zT[:, r, cols], zT[:, r, cols], rot[:, i % 2], ALU.add
                                        ).then_inc(s["rope_done"], 1)

                dve.wait_ge(s["state_set"], BASE + l + 1)
                step.link(v.memset(u[:, 0:2], 0.0))
                settle(dve, s["dve_passed"])
                with step.loop(CG, 9) as g:
                    dve.wait_ge(s["act_ev"], BASE + (l * NTILE + 6 + 3 * g + 3) * NCH + 6)
                    cw = [convw[:, ds(l, 1), ds(g, 1), j:j + 1].rearrange("p a b c -> p (a b c)") for j in range(3)]
                    sug = su[:, ds(g * NS, NS), :]
                    step.mark(v.tensor_tensor(u[:, 2:SEQ + 2], cbuf[:, 0:SEQ], hbuf[:, 0:SEQ], ALU.mult))
                    step.link(v.tensor_tensor(sug[:, :, 2], cbuf[:, SEQ:T], hbuf[:, SEQ:T], ALU.mult))
                    step.mark(v.tensor_copy(upo[:, ds(g, 1), :].rearrange("p a b -> p (a b)"), u[:, SEQ:SEQ + 2]))
                    accs = hbuf[:, SEQ:T]
                    step.mark(v.tensor_scalar(acc, u[:, 0:SEQ], cw[0], None, ALU.mult))
                    step.link(v.tensor_scalar(accs, sug[:, :, 0], cw[0], None, ALU.mult))
                    step.mark(v.scalar_tensor_tensor(acc, u[:, 1:SEQ + 1], cw[1], acc, ALU.mult, ALU.add))
                    step.link(v.scalar_tensor_tensor(accs, sug[:, :, 1], cw[1], accs, ALU.mult, ALU.add))
                    step.mark(v.scalar_tensor_tensor(acc, u[:, 2:SEQ + 2], cw[2], acc, ALU.mult, ALU.add))
                    step.link(v.scalar_tensor_tensor(accs, sug[:, :, 2], cw[2], accs, ALU.mult, ALU.add))
                    gTg = gT[:, ds(g, 1), :].rearrange("p a b -> p (a b)")
                    v.tensor_tensor(gTg[:, 0:SEQ], acc, bbuf[:, 0:SEQ], ALU.mult)
                    v.tensor_tensor(gTg[:, SEQ:T], accs, bbuf[:, SEQ:T], ALU.mult).then_inc(s["conv_done"], 1)

                def values(b, slot):
                    n = NB * l + b
                    dve.wait_ge(s["v_t"], BASE + n + 1)
                    dve.wait_ge(s["pv_mm"], BASE + n)
                    v.tensor_copy(vnat[:, slot], ps[:, 4, 0:P]).then_inc(s["v_ev"], 1)

                def max_of(b, mask):
                    n = NB * l + b
                    for h in range(NKV):
                        dve.wait_ge(s["s_mm"], BASE + 2 * n + h + 1)
                        step.link(v.scalar_tensor_tensor(
                            sS[:, h], ps[:, 2 * h:2 * h + 2, :].rearrange("p a (c k) -> p (a c) k", c=2), HD ** -0.5,
                            masks[:, mask:mask + 1, :].broadcast_to([P, QPK, 2 * P]), ALU.mult, ALU.add))
                        step.link(v.tensor_reduce(sm[:, h, 0], sS[:, h], AX.X, ALU.max))
                        sk = sinks[:, ds(l * NH + h * QPK, QPK)]
                        step.link(v.tensor_tensor(sm[:, h, 0], sm[:, h, 0], sk, ALU.max))
                        step.mark(v.tensor_scalar(sm[:, h, 1], sm[:, h, 0], -1.0, None, ALU.mult))
                        step.link(v.tensor_tensor(sm[:, h, 2], sk, sm[:, h, 0], ALU.subtract))
                        dve.sem_inc(s["sm_ready"], 1)

                def residual(b, slot, rows):
                    m = NT * l + b
                    dve.wait_ge(s["wo_mm"], BASE + m + 3)
                    dve.wait_ge(s["x1_ready"], BASE + m)
                    dve.wait_ge(s[f"xr_in{slot}"], BASE + 16 * ((5 - slot) * l + b // 2 + 1))
                    v.scalar_tensor_tensor(t1[0:rows], xres[0:rows, slot], ALPHA,
                                           ps[0:rows, 6:8, :].rearrange("p a b -> p (a b)"), ALU.mult, ALU.add
                                           ).then_inc(s["ln_add"], 1)
                    dve.wait_ge(s["ln_add"], BASE + m + 1)
                    moments(t1[0:rows], 0, rows, s["ln_stat"])

                def scaled(b, rows):
                    m = NT * l + b
                    dve.wait_ge(s["ln_hat"], BASE + m + 1)
                    v.tensor_tensor(t1[0:rows], t1[0:rows], lnp[0:rows, 0], ALU.mult).then_inc(s["ln_scaled"], 1)

                def normalise(b):
                    n = NB * l + b
                    dve.wait_ge(s["pt_ev"], BASE + 2 * n + 2)
                    dve.wait_ge(s["ot_mm"], BASE + n)
                    step.link(v.tensor_tensor(rl[:].rearrange("p (h j) -> p h j", h=NKV), sm[:, :, 3], sm[:, :, 4], ALU.add))
                    step.link(v.reciprocal(rl[:], rl[:]))
                    dve.wait_ge(s["pv_mm"], BASE + n + 1)
                    v.tensor_tensor(oS.rearrange("p (h d) -> p h d", h=NH), ps[:, 4, :].rearrange("p (h d) -> p h d", h=NH),
                                    rl[:].unsqueeze(2).broadcast_to([P, NH, HD]), ALU.mult).then_inc(s["o_norm"], 1)

                def x1t_evict(b, rows):
                    m = NT * l + b
                    dve.wait_ge(s["x1t_mm"], BASE + m + 1)
                    dve.wait_ge(s["rt_mm"], BASE + m)
                    v.tensor_copy(x1T[:, 4:8, 0:rows],
                                  ps[:, 7, :].rearrange("p (k t) -> p k t", k=4)[:, :, 0:rows]).then_inc(s["x1t_d"], 1)

                def logit(b, rows):
                    m = NT * l + b
                    dve.wait_ge(s["rt_mm"], BASE + m + 1)
                    v.tensor_tensor(logits[0:rows, ds(b, 1), :].rearrange("p a n -> p (a n)"), ps[0:rows, 5, 0:NR],
                                    br[0:rows, ds(l, 1), :].rearrange("p a n -> p (a n)"), ALU.add
                                    ).then_inc(s["lg_ev"], 1)

                def body(b, slot, mask, bq):
                    values(b, slot)
                    max_of(b, mask)
                    residual_at(b - 1, 1 - slot, bq)
                    scaled(b - 1, P)
                    normalise(b)
                    x1t_evict(b - 1, P)
                    logit(b - 1, P)

                def residual_at(b, slot, q):
                    m = NT * l + b
                    dve.wait_ge(s["wo_mm"], BASE + m + 3)
                    dve.wait_ge(s["x1_ready"], BASE + m)
                    dve.wait_ge(s[f"xr_in{slot}"], BASE + 16 * ((5 - slot) * l + q + 1))
                    v.scalar_tensor_tensor(t1[0:P], xres[0:P, slot], ALPHA,
                                           ps[0:P, 6:8, :].rearrange("p a b -> p (a b)"), ALU.mult, ALU.add
                                           ).then_inc(s["ln_add"], 1)
                    dve.wait_ge(s["ln_add"], BASE + m + 1)
                    moments(t1[0:P], 0, P, s["ln_stat"])

                values(0, 0)
                max_of(0, 0)
                normalise(0)
                settle(dve, s["dve_passed"])
                with step.loop(3, 2 * 14) as i:
                    body(2 * i + 1, 1, 2, i)
                    body(2 * i + 2, 0, 1, i)
                body(7, 1, 2, 3)

                dve.wait_ge(s["smp_s"], BASE + l + 1)
                sk = sinkc[:, ds(l, 1)]
                step.link(v.tensor_scalar(ss, ps[0:64, 0, 0:P + 1], HD ** -0.5, None, ALU.mult))
                step.link(v.tensor_reduce(smp[:, 0:1], ss, AX.X, ALU.max))
                step.link(v.tensor_tensor(smp[:, 0:1], smp[:, 0:1], sk, ALU.max))
                step.mark(v.tensor_scalar(smp[:, 1:2], smp[:, 0:1], -1.0, None, ALU.mult))
                v.tensor_tensor(smp[:, 2:3], sk, smp[:, 0:1], ALU.subtract).then_inc(s["smp_max"], 1)
                dve.wait_ge(s["smp_n"], BASE + l + 1)
                step.link(v.tensor_tensor(smp[:, 5:6], smp[:, 3:4], smp[:, 4:5], ALU.add))
                step.link(v.reciprocal(smp[:, 5:6], smp[:, 5:6]))
                step.link(v.tensor_scalar(ssn, ss, smp[:, 5:6], None, ALU.mult))
                v.tensor_scalar(diag, ident[0:64, 0:64], ssn[:, P:P + 1], None, ALU.mult).then_inc(s["smp_p"], 1)
                dve.wait_ge(s["smp_t"], BASE + l + 1)
                step.mark(v.tensor_copy(ptz.rearrange("p (b x) -> p b x", b=NS)[:, :, 0:NH],
                                        ps[:, 1, 0:64].rearrange("p (b h) -> p b h", b=NS)))
                step.mark(v.tensor_copy(pnew, ps[0:NS, 2, 0:64]))
                v.tensor_copy(vnew, ps[0:NS, 3, 0:P]).then_inc(s["smp_pt"], 1)
                dve.wait_ge(s["smp_o"], BASE + l + 1)
                step.link(v.tensor_scalar(osel, ps[0:64, 4, 0:HD], half_mask[:, 0:1], None, ALU.mult))
                v.scalar_tensor_tensor(osel, ps[0:64, 4, HD:P], half_mask[:, 1:2], osel, ALU.mult, ALU.add
                                       ).then_inc(s["smp_sel"], 1)
                dve.wait_ge(s["smp_ot"], BASE + l + 1)
                dve.wait_ge(s["wo_mm"], BASE + NT * l + 9)
                oT = ps[0:64, 1, 0:64].rearrange("p (b j two) -> p two j b", b=NS, two=2)
                step.mark(v.tensor_copy(mixT[0:64, 0, 0:4, 0:NS], oT[:, 0]))
                v.tensor_copy(mixT[64:128, 0, 0:4, 0:NS], oT[:, 1]).then_inc(s["smp_mix"], 1)

                residual(7, 1, P)
                scaled(7, P)
                x1t_evict(7, P)
                logit(7, P)
                residual(8, 0, NS)
                scaled(8, NS)
                x1t_evict(8, NS)
                logit(8, NS)

                def op(ins):
                    step.link(ins)

                def tt(out, in0, in1, o):
                    step.link(v.tensor_tensor(out, in0, in1, o))

                def ts(out, in0, c1, c2, o1, o2=ALU.bypass):
                    step.link(v.tensor_scalar(out, in0, c1, c2, o1, o2))

                def wide(ap, n):
                    return ap.broadcast_to([P, NT, n])

                def desc(n):
                    return rank_desc[:, NE - n:NE].unsqueeze(1).broadcast_to([P, NT, n])

                L, E, tmp, M, before, total, g7, prod, r9 = rt[0], (rt[1], rt[2]), rt[3], rt[4], rt[5], rt[6], rt[7], rt[8], rt[9]

                def first_max(values, n, top, place, onehot):
                    op(v.tensor_reduce(r9[:, :, top], values, AX.X, ALU.max))
                    tt(tmp[:, :, 0:n], values, wide(r9[:, :, top:top + 1], n), ALU.is_equal)
                    tt(tmp[:, :, 0:n], tmp[:, :, 0:n], desc(n), ALU.mult)
                    op(v.tensor_reduce(r9[:, :, place], tmp[:, :, 0:n], AX.X, ALU.max))
                    tt(onehot, desc(n), wide(r9[:, :, place:place + 1], n), ALU.is_equal)

                dve.wait_ge(s["lg_ev"], BASE + NT * (l + 1))
                dve.wait_ge(s["small_out"], BASE + 16 * 7 * (l + 1))
                gl = logits[:, :, 0:NG]
                first_max(gl, NG, 0, 1, g7[:, :, 4:8])
                tt(g7[:, :, 0:4], gl, wide(r9[:, :, 0:1], NG), ALU.subtract)
                ts(tmp[:, :, 0:4], g7[:, :, 4:8], BIG, -BIG, ALU.mult, ALU.add)
                tt(L.rearrange("p t (g e) -> p t g e", g=NG), logits[:, :, NG:NR].rearrange("p t (g e) -> p t g e", g=NG),
                   tmp[:, :, 0:4].unsqueeze(3).broadcast_to([P, NT, NG, NE_G]), ALU.add)
                first_max(L, NE, 2, 3, E[0])
                ts(prod, E[0], -BIG, None, ALU.mult)
                tt(L, L, prod, ALU.add)
                first_max(L, NE, 4, 5, E[1])
                v.tensor_tensor(g7[:, :, 8:9], r9[:, :, 4:5], r9[:, :, 2:3], ALU.subtract).then_inc(s["rk_soft"], 1)
                tt(M, E[0], E[1], ALU.add)
                tt(M, M, wide(valid[:].unsqueeze(2), NE), ALU.mult)
                step.link(v.memset(before[:, 0], 0.0))
                for t in range(NT - 1):
                    tt(before[:, t + 1], before[:, t], M[:, t], ALU.add)
                v.tensor_tensor(total[:, 0], before[:, NT - 1], M[:, NT - 1], ALU.add).then_inc(s["rk_m"], 1)
                dve.wait_ge(s["rk_exp"], BASE + l + 1)
                op(v.tensor_reduce(r9[:, :, 6], g7[:, :, 0:4], AX.X, ALU.add))
                ts(r9[:, :, 7], g7[:, :, 8], 1.0, None, ALU.add)
                tt(r9[:, :, 6], r9[:, :, 6], r9[:, :, 7], ALU.mult)
                gate = rk[:, 0]
                op(v.reciprocal(gate[:, 0:NT], r9[:, :, 6]))
                tt(gate[:, NT:2 * NT], gate[:, 0:NT], g7[:, :, 8], ALU.mult)
                dve.wait_ge(s["rk_c"], BASE + l + 1)
                ts(ovs[:, 0], ps[:, 5, 0:NE], 127.0, None, ALU.add)
                op(v.tensor_copy(rki[:, 0:NE], ovs[:, 0]))
                ts(rki[:, 0:NE], rki[:, 0:NE], 7, None, ALU.logical_shift_right)
                op(v.tensor_copy(ovs[:, 0], rki[:, 0:NE]))
                ts(ovs[:, 0], ovs[:, 0], -1.0, 0.0, ALU.add, ALU.max)
                op(v.tensor_tensor_scan(ovs[:, 1], ones[:, 0:NE], ovs[:, 0], 0.0, ALU.mult, ALU.add))
                tt(ovs[:, 2], ovs[:, 1], ovs[:, 0], ALU.subtract)
                tt(over_cmp[:], ovs[0:1, 1:2, :].broadcast_to([1, OVER, NE]),
                   iota[0:1, 0:OVER].unsqueeze(2).broadcast_to([1, OVER, NE]), ALU.is_le)
                op(v.tensor_reduce(over_f[:, 0:OVER], over_cmp[:], AX.X, ALU.add))
                ts(over_f[:, 0:OVER], over_f[:, 0:OVER], float(NE - 1), None, ALU.min)
                op(v.tensor_copy(over_f[:, OVER:OVER + 1], ovs[0:1, 1, NE - 1:NE]))
                op(v.tensor_copy(over_f[:, OVER + 1:OVER + 2], over_f[:, OVER + 2:OVER + 3]))
                op(v.tensor_copy(over[:], over_f[:]))
                op(v.scalar_tensor_tensor(over_f[:, OVER + 2:OVER + 3], over_f[:, OVER:OVER + 1], 1.0,
                                          over_f[:, OVER + 2:OVER + 3], ALU.min, ALU.add))
                rank, expert, base, hi, lo, col, low = (rk[:, n] for n in range(1, 8))
                for k in range(2):
                    c = slice(k * NT, (k + 1) * NT)
                    tt(prod, ps[:, 4, 0:NT * NE].rearrange("p (t e) -> p t e", t=NT), E[k], ALU.mult)
                    op(v.tensor_reduce(rank[:, c], prod, AX.X, ALU.add))
                    tt(prod, ovs[:, 2:3, :].broadcast_to([P, NT, NE]), E[k], ALU.mult)
                    op(v.tensor_reduce(base[:, c], prod, AX.X, ALU.add))
                    ts(expert[:, c], r9[:, :, 3 + 2 * k], -1.0, float(NE), ALU.mult, ALU.add)
                ri = rki[:, 0:2 * NT]
                op(v.tensor_copy(ri, rank))
                ts(ri, ri, 7, None, ALU.logical_shift_right)
                op(v.tensor_copy(hi, ri))
                op(v.scalar_tensor_tensor(lo, hi, -128.0, rank, ALU.mult, ALU.add))
                ts(low, hi, 1.0, None, ALU.min)
                tt(base, base, hi, ALU.add)
                tt(base, base, expert, ALU.subtract)
                op(v.scalar_tensor_tensor(base, base, float(NE - 1), low, ALU.add, ALU.mult))
                tt(col, base, expert, ALU.add)
                for k in range(2):
                    c = slice(k * NT, (k + 1) * NT)
                    tt(col[:, c], col[:, c], valid[:], ALU.mult)
                    op(v.scalar_tensor_tensor(col[:, c], valid[:], -1.0, col[:, c], ALU.add, ALU.add))
                for i in range(2 * NT):
                    dve.wait_ge(s["rk_inv"], BASE + 2 * NT * l + max(i - 1, 0))
                    step.mark(v.tensor_scalar(slot_of[:, i % 2], iota[:], lo[:, i:i + 1], None, ALU.is_equal))
                    for q, w in enumerate((tokens1, kscale, gate)):
                        ins = v.tensor_scalar(block_of[:, i % 2, q * NBLK:(q + 1) * NBLK], iota[:, 0:NBLK],
                                              col[:, i:i + 1], w[:, i:i + 1], ALU.is_equal, ALU.mult)
                        if q < 2:
                            step.mark(ins)
                    ins.then_inc(s["rk_r"], 1)
                dve.wait_ge(s["rk_inv"], BASE + 2 * NT * (l + 1))
                op(v.tensor_copy(inv[:].rearrange("p q n -> p (q n)"), ps[:, 0, 0:3 * NBLK]))
                skip, row = prod[:, 0:2, :].rearrange("p a b -> p (a b)")[:, 0:NBLK], tmp[:, 0:2, :].rearrange("p a b -> p (a b)")[:, 0:NBLK]
                ts(skip, inv[:, 0], 0.0, float(SKIP), ALU.is_equal, ALU.mult)
                op(v.scalar_tensor_tensor(row, inv[:, 0], -1.0, skip, ALU.add, ALU.add))
                op(v.tensor_copy(gidx[:], row))
                op(v.scalar_tensor_tensor(row, inv[:, 1], float(T), row, ALU.mult, ALU.add))
                v.tensor_copy(sidx[:], row).then_inc(s["idx_ready"], 1)

                def xg_evict(e, slot):
                    n = NE * l + e
                    dve.wait_ge(s["xg_mm"], BASE + n + 3)
                    dve.wait_ge(s["gu_mm"], BASE + 2 * n + 2)
                    v.tensor_copy(xgT[:, slot, 4:8].rearrange("p k t -> p (k t)"), ps[:, 1, :]).then_inc(s["xg_d"], 1)

                def hidden(e, slot):
                    n = NE * l + e
                    dve.wait_ge(s["dn_mm"], BASE + n + 1)
                    for q in range(2):
                        dve.wait_ge(s["silu"], BASE + 2 * n + q + 1)
                        v.tensor_tensor(hT[:, slot, 2 * q:2 * q + 2].rearrange("p f t -> p (f t)"),
                                        ps[:, 2 + 2 * slot + q, 2 * P:4 * P],
                                        sg[:, 2 * q:2 * q + 2].rearrange("p f t -> p (f t)"), ALU.mult
                                        ).then_inc(s["h_ready"], 1)

                def y_evict(e, slot, turn):
                    n = NE * l + e
                    dve.wait_ge(s["dn_mm"], BASE + n + 3)
                    dve.wait_ge(s["ys_free"], BASE + n + 1)
                    v.tensor_scalar(ys[:, slot, 512:DM], ps[:, 7, :], inv[:, 2, ds(e, 1)], None, ALU.mult
                                    ).then_inc(s["y_d"], 1)

                xg_evict(0, 0)
                settle(dve, s["dve_passed"])
                with dve.Fori(0, NE // 2 - 1) as i:
                    hidden(2 * i, 0)
                    xg_evict(2 * i + 1, 1)
                    y_evict(2 * i, 0, i)
                    hidden(2 * i + 1, 1)
                    xg_evict(2 * i + 2, 0)
                    y_evict(2 * i + 1, 1, i)
                i = NE // 2 - 1
                hidden(2 * i, 0)
                xg_evict(2 * i + 1, 1)
                y_evict(2 * i, 0, i)
                hidden(2 * i + 1, 1)
                y_evict(2 * i + 1, 1, i)

                settle(dve, s["dve_passed"])
                with dve.If(dve.value_load(over[0:1, OVER:OVER + 1], min_val=0, max_val=OVER) > 0):
                    settle(dve, s["dve_passed"])
                    with dve.Fori(0, OVER) as o:
                        n = OVER * l + o
                        dve.wait_ge(s["ov_silu"], BASE + n + 1)
                        v.tensor_tensor(hT[:, 0].rearrange("p f t -> p (f t)"), ps[:, 4, :],
                                        sg.rearrange("p f t -> p (f t)"), ALU.mult).then_inc(s["ov_h"], 1)
                        dve.wait_ge(s["ov_dn"], BASE + n + 1)
                        v.tensor_scalar(ys[:, 0], ps[:, 6:8, :].rearrange("p a b -> p (a b)"),
                                        inv[:, 2, ds(o + NE, 1)], None, ALU.mult).then_inc(s["ov_y"], 1)
                with dve.Else():
                    dve.sem_inc(s["ov_h"], OVER)
                    dve.sem_inc(s["ov_y"], OVER)

                def add2(t, slot, rows, turn):
                    m = NT * l + t
                    dve.wait_ge(s[f"l2_in{slot}"], BASE + 48 * ((5 - slot) * l + turn + 1))
                    dve.wait_ge(s["x2_ready"], BASE + NT * l + (t - 1 if not isinstance(t, int) else max(t - 1, 0)))
                    tv = t2[0:rows, slot]
                    step.link(v.scalar_tensor_tensor(tv, l2in[0:rows, slot, 2 * DM:], ALPHA, l2in[0:rows, slot, 0:DM],
                                                     ALU.mult, ALU.add))
                    v.tensor_tensor(tv, tv, l2in[0:rows, slot, DM:2 * DM], ALU.add).then_inc(s["l2_add"], 1)
                    dve.wait_ge(s["l2_add"], BASE + m + 1)
                    moments(tv, slot, rows, s["l2_stat"])

                def scaled2(t, slot, rows):
                    dve.wait_ge(s["l2_hat"], BASE + NT * l + t + 1)
                    v.tensor_tensor(t2[0:rows, slot], t2[0:rows, slot], lnp[0:rows, 2], ALU.mult
                                    ).then_inc(s["l2_scaled"], 1)

                add2(0, 0, P, 0)
                settle(dve, s["dve_passed"])
                with step.loop(3, 6) as i:
                    for n in range(2):
                        add2(2 * i + n + 1, 1 - n, P, i + n)
                        scaled2(2 * i + n, n, P)
                        xt_evict(NT * (l + 1) + 2 * i + n, n, (2 * i + n) * P, P)
                add2(7, 1, P, 3)
                scaled2(6, 0, P)
                xt_evict(NT * (l + 1) + 6, 0, 6 * P, P)
                add2(8, 0, NS, 4)
                scaled2(7, 1, P)
                xt_evict(NT * (l + 1) + 7, 1, 7 * P, P)
                scaled2(8, 0, NS)
                xt_evict(NT * (l + 1) + 8, 0, SEQ, NS)

        @block.gpsimd
        def _(pool):
            raise_to_base(pool, "gpsimd")
            g = nc.gpsimd
            step = Steps(pool, s["pool_step"], s["pool_passed"])
            pool.wait_ge(s["const_in"], BASE + 16 * N_CONST)
            pool.wait_ge(s["init"], BASE + 6)

            def inverse_std(rows, slot, done):
                r = slice(0, rows)
                step.link(g.tensor_scalar(rstd[r, slot, 1:2], mv[r, slot, 1:2], EPS, None, ALU.add))
                step.link(g.tensor_tensor(rstd[r, slot, 0:1], rstd[r, slot, 1:2], mhalf[r], ALU.pow))
                step.link(g.tensor_tensor(rstd[r, slot, 1:2], mv[r, slot, 0:1], rstd[r, slot, 0:1], ALU.mult))
                g.tensor_scalar(rstd[r, slot, 1:2], rstd[r, slot, 1:2], -1.0, None, ALU.mult).then_inc(done, 1)

            with step.loop(DEPTH, STEPS_POOL) as l:
                for r in range(5):
                    for ch in range(NCH):
                        cols = slice(ch * CH, (ch + 1) * CH)
                        pool.wait_ge(s["act_ev"], BASE + (l * NTILE + r) * NCH + ch + 1 + 6)
                        g.tensor_tensor(zT[:, r, cols], ztmp[:, r % 2, cols], cosT[:, cols], ALU.mult
                                        ).then_inc(s["cos_done"], 1)
                pool.wait_ge(s["state_in"], BASE + 16 * (l + 1))
                settle(pool, s["pool_passed"])
                g.tensor_copy(su[:, :, 0:2], st[:]).then_inc(s["state_set"], 1)

                pool.wait_ge(s["conv_done"], BASE + CG * (l + 1))
                pool.wait_ge(s["rope_done"], BASE + 15 * (l + 1))
                pool.wait_ge(s["act_ev"], BASE + (l + 1) * NTILE * NCH + 6)

                def stage(b, slot):
                    n = NB * l + b
                    pool.wait_ge(s["s_mm"], BASE + 2 * n)
                    settle(pool, s["pool_passed"])
                    step.mark(g.tensor_copy(qs[:, slot], zT[:, 1:5, ds(b * P, P)]))
                    step.mark(g.tensor_copy(kwin[:, slot * P:(slot + 1) * P], zT[:, 0, ds(b * P, P)]))
                    step.link(g.tensor_copy(vs, zT[:, 5, ds(b * P, P)]))
                    pool.sem_inc(s["stage_done"], 1)

                def stage_gate(b, slot, cols):
                    m = NT * l + b
                    pool.wait_ge(s["wo_mm"], BASE + m + 1)
                    settle(pool, s["pool_passed"])
                    g.tensor_copy(mixT[:, slot, 4:8, 0:cols], gT[:, :, ds(b * P, cols)]).then_inc(s["gate_staged"], 1)

                def finish_at(b, slot, rows, turn):
                    m = NT * l + b
                    pool.wait_ge(s["ln_stat"], BASE + m + 1)
                    settle(pool, s["pool_passed"])
                    inverse_std(rows, 0, s["ln_rstd"])
                    pool.wait_ge(s["ln_scaled"], BASE + m + 1)
                    pool.wait_ge(s["x1t_mm"], BASE + m)
                    pool.wait_ge(s[f"x1_out{slot}"], BASE + 16 * ((5 - slot) * l + turn))
                    g.tensor_tensor(x1[0:rows, slot], t1[0:rows], lnp[0:rows, 1], ALU.add).then_inc(s["x1_ready"], 1)

                pool.wait_ge(s["lnp_in"], BASE + 16 * (l + 1))
                stage(0, 0)
                stage_gate(0, 0, P)
                with step.loop(3, 2 * 6) as i:
                    for n in range(2):
                        stage(2 * i + n + 1, 1 - n)
                        stage_gate(2 * i + n + 1, 1 - n, P)
                        finish_at(2 * i + n, n, P, i)
                stage(7, 1)
                stage_gate(7, 1, P)
                finish_at(6, 0, P, 3)

                pool.wait_ge(s["smp_in"], BASE + 32 * (l + 1))
                settle(pool, s["pool_passed"])
                step.mark(g.memset(ptz, 0.0))
                step.mark(g.tensor_copy(kTs[:, :, P], zT[:, 0, SEQ:T]))
                step.link(g.memset(qz, 0.0))
                for h in range(NKV):
                    ins = g.tensor_copy(
                        qz[h * HD:(h + 1) * HD].rearrange("p (b x) -> p b x", b=NS)[:, :, h * QPK:(h + 1) * QPK],
                        zT[h * HD:(h + 1) * HD, 1:5, SEQ:T].rearrange("p j b -> p b j"))
                    step.link(ins)
                pool.sem_inc(s["smp_q"], 1)
                stage_gate(8, 0, NS)
                finish_at(7, 1, P, 3)
                finish_at(8, 0, NS, 4)

                def gather(e, slot, turn):
                    n = NE * l + e
                    pool.wait_ge(s["xg_mm"], BASE + n + 1)
                    settle(pool, s["pool_passed"])
                    step.link(g.tensor_copy(gcol[:, slot:slot + 1], gidx[:, ds(e, 1)]))
                    g.indirect_dma_start(out=xg[:, slot], out_offset=None, in_=a["xs1"],
                                         in_offset=bass.IndirectOffsetOnAxis(ap=gcol[:, slot:slot + 1], axis=0),
                                         bounds_check=T - 1, oob_is_err=False).then_inc(s[f"xg_in{slot}"], 16)

                def scatter(e, slot, turn):
                    n = NE * l + e
                    if turn is not None:
                        pool.wait_ge(s[f"sc_out{slot}"], 16 * (NE // 2 * l + turn))
                        settle(pool, s["pool_passed"])
                    step.link(g.tensor_copy(scol[:, slot:slot + 1], sidx[:, ds(e, 1)]))
                    pool.sem_inc(s["ys_free"], 1)
                    pool.wait_ge(s["y_a"], BASE + n + 1)
                    pool.wait_ge(s["y_d"], BASE + n + 1)
                    settle(pool, s["pool_passed"])
                    g.indirect_dma_start(out=a["ytok"].rearrange("k t d -> (k t) d"),
                                         out_offset=bass.IndirectOffsetOnAxis(ap=scol[:, slot:slot + 1], axis=0),
                                         in_=ys[:, slot], in_offset=None,
                                         bounds_check=2 * T - 1, oob_is_err=False).then_inc(s[f"sc_out{slot}"], 16)

                pool.wait_ge(s["idx_ready"], BASE + l + 1)
                pool.wait_ge(s["x1_out0"], BASE + 16 * 5 * (l + 1))
                pool.wait_ge(s["x1_out1"], BASE + 16 * 4 * (l + 1))
                pool.wait_ge(s["smp_mix"], BASE + l + 1)
                pool.wait_ge(s["wo_mm"], BASE + NT * (l + 1) + 2)
                gather(0, 0, 0)
                gather(1, 1, 0)
                for slot in range(2):
                    scatter(slot, slot, None)
                    gather(slot + 2, slot, 1)
                with step.loop(NE // 2 - 2, 4) as i:
                    for slot in range(2):
                        scatter(2 * i + slot + 2, slot, i + 1)
                        gather(2 * i + slot + 4, slot, i + 2)
                for slot in range(2):
                    scatter(NE - 2 + slot, slot, NE // 2 - 1)

                settle(pool, s["pool_passed"])
                with pool.If(pool.value_load(over[0:1, OVER:OVER + 1], min_val=0, max_val=OVER) > 0):
                    pool.wait_ge(s["xg_mm"], BASE + NE * (l + 1) + 2)
                    for slot in range(2):
                        pool.wait_ge(s[f"sc_out{slot}"], 16 * (NE // 2) * (l + 1))
                    settle(pool, s["pool_passed"])
                    before = pool.value_load(over[0:1, OVER + 1:OVER + 2], min_val=0, max_val=DEPTH - 1)
                    with pool.Fori(0, OVER) as o:
                        n = OVER * l + o
                        sent = 16 * (OVER * before + o + 1)
                        pool.wait_ge(s["ov_xt"], BASE + n)
                        settle(pool, s["pool_passed"])
                        g.tensor_copy(gcol[:, 0:1], gidx[:, ds(o + NE, 1)]).then_inc(s["ov_col"], 1)
                        g.tensor_copy(scol[:, 0:1], sidx[:, ds(o + NE, 1)]).then_inc(s["ov_col"], 1)
                        pool.wait_ge(s["ov_col"], BASE + 2 * (n + 1))
                        settle(pool, s["pool_passed"])
                        g.indirect_dma_start(out=xg[:, 0], out_offset=None, in_=a["xs1"],
                                             in_offset=bass.IndirectOffsetOnAxis(ap=gcol[:, 0:1], axis=0),
                                             bounds_check=T - 1, oob_is_err=False).then_inc(s["ov_x"], 16)
                        pool.wait_ge(s["ov_x"], sent)
                        pool.sem_inc(s["ov_xin"], 1)
                        pool.wait_ge(s["ov_y"], BASE + n + 1)
                        settle(pool, s["pool_passed"])
                        g.indirect_dma_start(out=a["ytok"].rearrange("k t d -> (k t) d"),
                                             out_offset=bass.IndirectOffsetOnAxis(ap=scol[:, 0:1], axis=0),
                                             in_=ys[:, 0], in_offset=None,
                                             bounds_check=2 * T - 1, oob_is_err=False).then_inc(s["ov_sc"], 16)
                        pool.wait_ge(s["ov_sc"], sent)
                        pool.sem_inc(s["ov_out"], 1)
                with pool.Else():
                    pool.sem_inc(s["ov_col"], 2 * OVER)
                    pool.sem_inc(s["ov_xin"], OVER)
                    pool.sem_inc(s["ov_out"], OVER)

                def finish2(t, slot, rows, turn):
                    m = NT * l + t
                    pool.wait_ge(s["l2_stat"], BASE + m + 1)
                    settle(pool, s["pool_passed"])
                    inverse_std(rows, slot, s["l2_rstd"])
                    pool.wait_ge(s["l2_scaled"], BASE + m + 1)
                    pool.wait_ge(s["xt_mm"], BASE + NT * (l + 1) + t + 1)
                    pool.wait_ge(s[f"x2_out{slot}"], BASE + 16 * ((5 - slot) * l + turn))
                    g.tensor_tensor(x2[0:rows, slot], t2[0:rows, slot], lnp[0:rows, 3], ALU.add).then_inc(s["x2_ready"], 1)

                with step.loop(4, 6) as i:
                    for slot in range(2):
                        finish2(2 * i + slot, slot, P, i)
                finish2(8, 0, NS, 4)


def kernel(**inputs):
    import numpy as _np
    import concourse.bacc as _bacc
    from concourse.bass_utils import run_bass_kernel_spmd as _run

    f = {n: _np.asarray(v) for n, v in inputs.items()}
    L = DEPTH
    f32 = _np.float32
    A, KV, C = NH * HD, NKV * HD, CG * P
    cols = [_np.arange(A, A + KV)]
    for j in range(QPK):
        cols.append(_np.concatenate([_np.arange(h * HD, (h + 1) * HD) for h in (j, j + QPK)]))
    cols.append(_np.arange(A + KV, A + 2 * KV))
    at_b, at_c, at_h = A + 2 * KV, A + 2 * KV + C, A + 2 * KV + 2 * C
    for g in range(CG):
        cols += [_np.arange(o + g * P, o + (g + 1) * P) for o in (at_c, at_h, at_b)]
    w_in = f["w_in"][:, :, _np.concatenate(cols)].reshape(L, KD, P, NTILE, P).transpose(0, 3, 2, 1, 4)

    pos = _np.concatenate([_np.arange(SEQ), _np.full(NS, PAST)]).astype(f32)
    freq = (f32(10000.0) ** (-_np.arange(HD // 2, dtype=f32) / f32(HD // 2))).astype(f32)
    ang = (pos[None, :] * freq[_np.arange(P) % (HD // 2)][:, None]).astype(f32)
    swap = _np.zeros((P, P), f32)
    for m in range(P):
        d = m % HD
        swap[(m + HD // 2) if d < HD // 2 else (m - HD // 2), m] = -1.0 if d < HD // 2 else 1.0
    q_at, k_at = _np.arange(P)[:, None], _np.arange(P)[None, :]
    cur = _np.where(k_at <= q_at, 0.0, -BIG)
    prev = _np.where(k_at >= q_at, 0.0, -BIG)
    none = _np.full((P, P), -BIG)
    masks = _np.stack([_np.concatenate(m, 1) for m in ((cur, none), (cur, prev), (prev, cur))], 1)
    tok = _np.arange(NT)[None, :] * P + _np.arange(P)[:, None]
    arrays = {
        "x_all": _np.concatenate([f["x_prompt"].reshape(SEQ, DM), f["x_sample"].reshape(NS, DM)]),
        "w_in": w_in.reshape(L, NTILE, P, DM),
        "w_o": f["w_o"],
        "sinks": f["attn_sinks"].reshape(-1),
        "sinkc": _np.tile(f["attn_sinks"], (1, NS)).T,
        "conv_w": f["conv_w"].reshape(L, 3, CG, P).transpose(3, 0, 2, 1),
        "ln": _np.stack([f[n] for n in ("ln1_g", "ln1_b", "ln2_g", "ln2_b")], 1).reshape(L, 4 * DM),
        "w_r": _np.concatenate([f["w_router_group"], f["w_router_expert"]], 2),
        "b_r": _np.concatenate([f["b_router_group"], f["b_router_expert"]], 1),
        "w_gate": f["w_gate"], "w_up": f["w_up"], "w_down": f["w_down"],
        "cache_kT": f["cache_k_win"].reshape(L, NS, P, P).transpose(0, 3, 1, 2),
        "cache_v": f["cache_v_win"].reshape(L, NS, P, P),
        "state": f["state_conv"].reshape(L, NS, 2, CG, P).transpose(0, 4, 3, 1, 2).reshape(L, P, CG * NS, 2),
        "c_ident": _np.eye(P, dtype=f32),
        "c_rot": swap,
        "c_upper": _np.triu(_np.ones((P, P), f32), 1),
        "c_iota": _np.tile(_np.arange(P, dtype=f32), (P, 1)),
        "c_masks": masks.astype(f32),
        "c_cos": _np.cos(ang), "c_sin": _np.sin(ang),
        "c_desc": _np.tile(_np.arange(NE, 0, -1, dtype=f32), (P, 1)),
        "c_tok1": _np.tile(tok + 1, (1, 2)).astype(f32),
        "c_k": _np.tile(_np.repeat(_np.arange(2, dtype=f32), NT), (P, 1)),
        "c_valid": (tok < T).astype(f32),
        "c_sel8": _np.repeat(_np.eye(NS, dtype=f32), NH, 0),
        "c_half": _np.stack([_np.arange(64) % NH < QPK, _np.arange(64) % NH >= QPK], 1).astype(f32),
    }
    outs = {
        "y_all": (L + 1, T, DM), "o_kp": (L, P, P), "o_vp": (L, P, P), "o_ks": (L, P, NS, P),
        "o_vs": (L, NS, P, P), "o_cp": (L, P, CG, 2), "o_cs": (L, P, CG * NS, 3),
    }
    nc = _bacc.Bacc("TRN2", target_bir_lowering=False, num_devices=1)
    aps, feed = {}, {}
    for name, v in arrays.items():
        feed[f"in_{name}"] = v = _np.ascontiguousarray(v)
        aps[name] = nc.dram_tensor(f"in_{name}", v.shape, mybir.dt.from_np(v.dtype), kind="ExternalInput").ap()
    for name, shape in outs.items():
        aps[name] = nc.dram_tensor(f"out_{name}", shape, F32, kind="ExternalOutput").ap()
    aps["xs1"] = nc.dram_tensor("xs1", (T, DM), F32).ap()
    aps["ytok"] = nc.dram_tensor("ytok", (2, T, DM), F32).ap()
    build(nc, aps)
    r = _run(nc, [feed], core_ids=[0]).results[0]
    o = {name: r[f"out_{name}"] for name in outs}

    def windows(t):
        return _np.ascontiguousarray(t.transpose(0, 2, 1)).reshape(L, 1, P, NKV, HD)

    y = o["y_all"][L]
    return (
        y[:SEQ].reshape(1, SEQ, DM), y[SEQ:].reshape(NS, 1, DM), windows(o["o_kp"]), windows(o["o_vp"]),
        _np.ascontiguousarray(o["o_cp"].transpose(0, 3, 2, 1)).reshape(L, 1, 2, C),
        _np.ascontiguousarray(o["o_ks"].transpose(0, 2, 3, 1)).reshape(L, NS, P, NKV, HD),
        o["o_vs"].reshape(L, NS, P, NKV, HD),
        _np.ascontiguousarray(o["o_cs"].reshape(L, P, CG, NS, 3)[..., 1:].transpose(0, 3, 4, 2, 1)).reshape(L, NS, 2, C),
    )
```

```python
from contextlib import ExitStack, contextmanager

import numpy as np

import concourse.bass as bass
from concourse import mybir

F32 = mybir.dt.float32
I32 = mybir.dt.int32
ALU = mybir.AluOpType
ACT = mybir.ActivationFunctionType
AX = mybir.AxisListType

P = 128
DM = 1024
KD = DM // P
DEPTH = 2
SEQ = 1024
NS = 8
T = SEQ + NS
NB = SEQ // P
NT = NB + 1
HD, NH, NKV = 64, 8, 2
QPK = NH // NKV
NG, NE_G = 4, 8
NE = NG * NE_G
DE = 512
FD = DE // P
NR = NG + NE
CG = 4
NTILE = 6 + 3 * CG
CH = T // 3
NCH = 3
OVER = (2 * T) // P
NBLK = NE + OVER
ALPHA = (2 * DEPTH) ** 0.25
EPS = 1e-5
STEPS_LAYER = 275
STEPS_POOL = 147
BIG = 1e30
BASE = 2
BY_POOL = ("xg_in0", "xg_in1", "sc_out0", "sc_out1", "ov_x", "ov_sc")
SKIP = 1 << 20
PAST = 4096


def settle(eng, passed):
    eng.sem_inc(passed, 1)


class Steps:

    def __init__(self, eng, sem, passed=None):
        self.eng, self.sem, self.base, self.n, self.passed = eng, sem, 0, 0, passed

    def mark(self, ins):
        ins.then_inc(self.sem, 1)
        self.n += 1

    def wait(self):
        self.eng.wait_ge(self.sem, self.base + self.n)
        if self.passed is not None:
            settle(self.eng, self.passed)

    def link(self, ins):
        self.mark(ins)
        self.wait()

    @contextmanager
    def loop(self, count, per):
        base, n = self.base, self.n
        if self.passed is not None:
            settle(self.eng, self.passed)
        with self.eng.Fori(0, count) as i:
            self.base, self.n = base + n + i * per, 0
            yield i
            assert self.n == per, self.n
        self.base, self.n = base, n + count * per


def build(nc, a):
    ctx = ExitStack()
    with ctx:
        def sb(name, shape, dt=F32):
            return ctx.enter_context(nc.sbuf_tensor(name, shape, dt))

        def sem(name):
            return ctx.enter_context(nc.semaphore(name))

        def ds(i, n):
            return bass.ds(i, n)

        ident = sb("ident", [P, P])
        rotm = sb("rotm", [P, P])
        ones = sb("ones", [P, P])
        upper = sb("upper", [P, P])
        iota = sb("iota", [P, P])
        masks = sb("masks", [P, 3, 2 * P])
        cosT = sb("cosT", [P, T])
        sinT = sb("sinT", [P, T])
        rank_desc = sb("rank_desc", [P, NE])
        tokens1 = sb("tokens1", [P, 2 * NT])
        kscale = sb("kscale", [P, 2 * NT])
        valid = sb("valid", [P, NT])
        sel8 = sb("sel8", [64, NS])
        half_mask = sb("half_mask", [64, 2])
        sinks = sb("sinks", [P, DEPTH * NH])
        sinkc = sb("sinkc", [64, DEPTH])
        convw = sb("convw", [P, DEPTH, CG, 3])
        wr = sb("wr", [P, DEPTH, KD, NR])
        br = sb("br", [P, DEPTH, NR])
        lnp = sb("lnp", [P, 4, DM])
        mhalf = sb("mhalf", [P, 1])
        kwin = sb("kwin", [P, 2 * P])
        vnat = sb("vnat", [P, 2, P])
        logits = sb("logits", [P, NT, NR])
        inv = sb("inv", [P, 3, NBLK])
        gidx = sb("gidx", [P, NBLK], I32)
        sidx = sb("sidx", [P, NBLK], I32)
        gcol = sb("gcol", [P, 2], I32)
        scol = sb("scol", [P, 2], I32)
        rki = sb("rki", [P, 2 * NT + NE], I32)
        over_cmp = sb("over_cmp", [1, OVER, NE])
        over_f = sb("over_f", [1, OVER + 3])
        over = sb("over", [1, OVER + 3], I32)
        stat = sb("stat", [P, 12])
        mv = sb("mv", [P, 2, 2])
        rstd = sb("rstd", [P, 2, 2])
        sm = sb("sm", [P, 2, 5, QPK])
        rl = sb("rl", [P, NH])
        smp = sb("smp", [64, 8])
        su = sb("su", [P, CG * NS, 3])
        st = sb("st", [P, CG * NS, 2])
        upo = sb("upo", [P, CG, 2])
        arena = sb("arena", [P, 39800])

        def at(off, *shape, parts=P):
            n = int(np.prod(shape))
            v = arena[0:parts, off:off + n]
            if len(shape) == 2:
                return v.rearrange("p (a b) -> p a b", a=shape[0])
            if len(shape) == 4:
                return v.rearrange("p (a b c d) -> p a b c d", a=shape[0], b=shape[1], c=shape[2])
            if len(shape) == 3:
                return v.rearrange("p (a b c) -> p a b c", a=shape[0], b=shape[1])
            return v

        xT = at(0, KD, T)
        zT = at(8256, 6, T)
        gT = at(14448, CG, T)
        wring = at(18576, 3, DM)
        ztmp = at(21648, 2, T)
        rot = at(23712, 2, CH)
        cbuf, hbuf, bbuf = at(24400, T), at(25432, T), at(26464, T)
        u = at(27496, SEQ + 2)
        acc = at(28528, SEQ)
        sS = at(0, 2, QPK, 2 * P)
        pT = at(2048, 2, QPK, 2, P)
        mixT = at(4096, 2, KD, P)
        x1T = at(6144, KD, P)
        t1 = at(7168, DM)
        qs = at(18576, 2, 4, P)
        vs = at(19600, P)
        oS = at(19728, NH * HD)
        xres = at(20240, 2, DM)
        x1 = at(22288, 2, DM)
        qz = at(24400, NS * 72)
        ptz = at(24976, NS * 72)
        ss = at(25552, P + 1, parts=64)
        ssn = at(25688, P + 1, parts=64)
        diag = at(25824, 64, parts=64)
        pnew = at(25888, 64, parts=NS)
        vnew = at(25952, P, parts=NS)
        osel = at(26080, 64, parts=64)
        wo = at(29552, KD, DM)
        kTs = at(37744, NS, P + 1)
        vS = at(38776, NS, P)
        rt = [at(33040 + 288 * n, NT, NE) for n in range(10)]
        slot_of = at(26704, 2 * NT, P)
        block_of = at(29552, 2 * NT, 3 * NBLK)
        rk = at(36464, 12, 2 * NT)
        ovs = at(36680, 4, NE)
        wg = (at(8256, KD, DE), at(0, KD, DE))
        wu = (at(12352, KD, DE), at(4096, KD, DE))
        wd = (at(16448, FD, DM), at(20544, FD, DM))
        xg = at(24656, 2, DM)
        xgT = at(26704, 2, KD, P)
        sg = at(28752, FD, P)
        hT = at(29264, 2, FD, P)
        ys = at(30288, 2, DM)
        l2in = at(8256, 2, 3 * DM)
        t2 = at(21648, NT, DM)
        x2 = at(16448, 2, DM)

        def t2_of(t, rows):
            return t2[0:rows, ds(t, 1), :].rearrange("p a d -> p (a d)")

        ps = ctx.enter_context(nc.psum_tensor("ps", [P, 8, 512], F32))

        s = {n: sem(n) for n in (
            "const_in", "init", "copied", "ident_in", "xin0", "xin1", "xt_mm", "xt_a", "xt_d", "x2_ready", "x2_out0",
            "x2_out1", "w_in0", "w_in1", "w_in2", "proj_mm", "act_ev", "rot_mm", "rot_used",
            "cos_done", "rope_done", "conv_done", "state_in", "state_set", "stage_done", "gate_staged", "v_t", "v_ev",
            "s_mm", "sm_ready", "p_ready", "pt_mm", "pt_ev", "pv_mm", "o_norm", "ot_mm", "ot_ev", "wo_in",
            "wo_mm", "xr_in0", "xr_in1", "ln_stat", "ln_rstd", "ln_hat", "ln_scaled", "ln_add", "x1_ready",
            "x1_out0", "x1_out1", "x1t_mm", "x1t_a", "x1t_d", "rt_mm", "lg_ev", "lnp_in", "smp_in",
            "smp_q", "smp_s", "smp_max", "smp_p", "smp_n", "smp_t", "smp_pt", "smp_o", "smp_sel", "smp_ot", "smp_mix",
            "small_out", "rk_m", "rk_c", "rk_r", "rk_inv", "idx_ready",
            "wg_in0", "wg_in1", "wu_in0", "wu_in1", "wd_in0", "wd_in1", "xg_in0", "xg_in1", "xg_mm",
            "xg_a", "xg_d", "gu_mm", "silu", "h_ready", "dn_mm", "y_a", "y_d", "sc_out0", "sc_out1",
            "l2_in0", "l2_in1", "l2_add", "l2_stat", "l2_rstd", "l2_hat", "l2_scaled", "dve_step", "pool_step",
            "pe_passed", "dve_passed", "pool_passed", "sp_passed", "rk_exp", "rk_soft",
            "ys_free", "ov_xin", "ov_out", "ov_w", "ov_x", "ov_col", "ov_xt", "ov_xa", "ov_gu", "ov_silu", "ov_h", "ov_dn", "ov_y", "ov_sc")}

        N_CONST = 19
        block = ctx.enter_context(nc.Block())

        SIGNALS = {
            "sync": (
                "const_in", "copied", "ident_in", "l2_in0", "l2_in1", "lnp_in", "ov_w", "small_out", "smp_in", "state_in", "w_in0",
                "w_in1", "w_in2", "wd_in0", "wd_in1", "wg_in0", "wg_in1", "wo_in", "wu_in0", "wu_in1", "x1_out0",
                "x1_out1", "x2_out0", "x2_out1", "xin0", "xin1", "xr_in0", "xr_in1"),
            "tensor": (
                "dn_mm", "gu_mm", "ot_mm", "ov_dn", "ov_gu", "ov_xt", "proj_mm", "pt_mm", "pv_mm", "rk_c", "rk_inv",
                "rot_mm", "rt_mm", "s_mm", "smp_o", "smp_ot", "smp_s", "smp_t", "v_t", "wo_mm", "x1t_mm", "xg_mm",
                "xt_mm"),
            "scalar": (
                "act_ev", "l2_hat", "ln_hat", "ot_ev", "ov_silu", "ov_xa", "p_ready", "pt_ev", "rk_exp", "silu",
                "smp_n", "x1t_a", "xg_a", "xt_a", "y_a"),
            "vector": (
                "conv_done", "h_ready", "idx_ready", "init", "l2_add", "l2_scaled", "l2_stat", "lg_ev", "ln_add",
                "ln_scaled", "ln_stat", "o_norm", "ov_h", "ov_y", "rk_m", "rk_r", "rk_soft", "rope_done",
                "rot_used", "sm_ready", "smp_max", "smp_mix", "smp_p", "smp_pt", "smp_sel", "v_ev", "x1_ready", "x1t_d", "xg_d",
                "xt_d", "y_d"),
            "gpsimd": (
                "cos_done", "gate_staged", "l2_rstd", "ln_rstd", "ov_col", "ov_out", "ov_xin", "smp_q",
                "stage_done", "state_set", "x2_ready", "ys_free"),
        }

        def raise_to_base(eng, name):
            for n in SIGNALS[name]:
                eng.sem_inc(s[n], BASE)

        @block.sync
        def _(sp):
            raise_to_base(sp, "sync")
            consts = [
                (rotm, a["c_rot"]), (upper, a["c_upper"]), (iota, a["c_iota"]),
                (masks, a["c_masks"]), (cosT, a["c_cos"]), (sinT, a["c_sin"]), (rank_desc, a["c_desc"]),
                (tokens1, a["c_tok1"]), (kscale, a["c_k"]), (valid, a["c_valid"]), (sel8, a["c_sel8"]),
                (half_mask, a["c_half"]),
                (sinks, a["sinks"].partition_broadcast(P)), (sinkc, a["sinkc"]), (convw, a["conv_w"]),
            ]
            for l in range(DEPTH):
                consts.append((wr[:, l], a["w_r"][l].rearrange("(k p) n -> p k n", p=P)))
                consts.append((br[:, l], a["b_r"][l].partition_broadcast(P)))
            assert len(consts) == N_CONST, len(consts)

            def x_tile(t, slot, rows):
                sp.dma_start(x2[0:rows, slot], a["x_all"][ds(t * P, rows), :]).then_inc(s[f"xin{slot}"], 16)

            sp.dma_start(ident[:], a["c_ident"]).then_inc(s["ident_in"], 16)
            x_tile(0, 0, P)
            x_tile(1, 1, P)
            settle(sp, s["sp_passed"])
            with sp.Fori(0, 3) as i:
                for slot in range(2):
                    sp.wait_ge(s["xt_mm"], BASE + 2 * i + slot + 3)
                    x_tile(2 * i + slot + 2, slot, P)
            sp.wait_ge(s["xt_mm"], BASE + 7 + 2)
            x_tile(8, 0, NS)

            def w_tile(c, slot):
                sp.wait_ge(s["proj_mm"], BASE + c * NCH)
                settle(sp, s["sp_passed"])
                sp.dma_start(wring[:, slot], a["w_in"][c]).then_inc(s[f"w_in{slot}"], 16)

            for slot in range(3):
                sp.dma_start(wring[:, slot], a["w_in"][slot]).then_inc(s[f"w_in{slot}"], 16)
            for dst, src in consts:
                sp.dma_start(dst if isinstance(dst, bass.AP) else dst[:], src).then_inc(s["const_in"], 16)
            sp.dma_start(a["y_all"][0], a["x_all"]).then_inc(s["copied"], 16)

            with sp.Fori(0, DEPTH) as l:
                sp.wait_ge(s["x2_ready"], BASE + 9 * l)
                sp.wait_ge(s["x1_ready"], BASE + 9 * l)
                settle(sp, s["sp_passed"])

                sp.dma_start(st[:], a["state"][l]).then_inc(s["state_in"], 16)
                sp.dma_start(lnp[:].rearrange("p a d -> p (a d)"), a["ln"][l].partition_broadcast(P)
                             ).then_inc(s["lnp_in"], 16)
                sp.dma_start(kTs[:, :, 0:P], a["cache_kT"][l]).then_inc(s["smp_in"], 16)
                sp.dma_start(vS, a["cache_v"][l].rearrange("b s d -> s b d")).then_inc(s["smp_in"], 16)
                sp.dma_start(wo, a["w_o"][l].rearrange("(k p) n -> p k n", p=P)).then_inc(s["wo_in"], 16)
                settle(sp, s["sp_passed"])
                with sp.Fori(0, NTILE // 3 - 1) as i:
                    for slot in range(3):
                        w_tile(NTILE * l + 3 * i + slot + 3, slot)

                def res_in(b, slot, rows, after):
                    sp.wait_ge(s["ln_add"], BASE + after)
                    settle(sp, s["sp_passed"])
                    sp.dma_start(xres[0:rows, slot], a["y_all"][l, ds(b * P, rows), :]
                                 ).then_inc(s[f"xr_in{slot}"], 16)

                def x1_out(b, slot, rows):
                    sp.wait_ge(s["x1_ready"], BASE + NT * l + b + 1)
                    settle(sp, s["sp_passed"])
                    sp.dma_start(a["xs1"][ds(b * P, rows), :], x1[0:rows, slot]).then_inc(s[f"x1_out{slot}"], 16)

                sp.wait_ge(s["copied"], BASE + 16)
                sp.wait_ge(s["conv_done"], BASE + (l + 1) * CG)
                sp.wait_ge(s["stage_done"], BASE + NB * l + 1)
                res_in(0, 0, P, NT * l)
                res_in(1, 1, P, NT * l)
                settle(sp, s["sp_passed"])
                with sp.Fori(0, 3) as i:
                    for slot in range(2):
                        res_in(2 * i + slot + 2, slot, P, NT * l + 2 * i + slot + 1)
                        x1_out(2 * i + slot, slot, P)
                sp.wait_ge(s["smp_mix"], BASE + l + 1)
                settle(sp, s["sp_passed"])
                sp.wait_ge(s["stage_done"], BASE + NB * (l + 1))
                settle(sp, s["sp_passed"])
                sp.dma_start(a["o_kp"][l], zT[:, 0, SEQ - P:SEQ]).then_inc(s["small_out"], 16)
                sp.dma_start(a["o_vp"][l], zT[:, 5, SEQ - P:SEQ]).then_inc(s["small_out"], 16)
                sp.dma_start(a["o_ks"][l], kTs[:, :, 1:P + 1]).then_inc(s["small_out"], 16)
                sp.dma_start(a["o_vs"][l, :, 0:P - 1, :].rearrange("b s d -> s b d"), vS[1:P]
                             ).then_inc(s["small_out"], 16)
                sp.dma_start(a["o_vs"][l, :, P - 1, :], vnew).then_inc(s["small_out"], 16)
                sp.dma_start(a["o_cp"][l], upo[:]).then_inc(s["small_out"], 16)
                sp.dma_start(a["o_cs"][l], su[:]).then_inc(s["small_out"], 16)

                def gate_up_in(e, slot):
                    sp.wait_ge(s["gu_mm"], BASE + 2 * (NE * l + e) + 2)
                    settle(sp, s["sp_passed"])
                    sp.dma_start(wg[slot], a["w_gate"][l, e].rearrange("(k p) f -> p k f", p=P)
                                 ).then_inc(s[f"wg_in{slot}"], 16)
                    sp.dma_start(wu[slot], a["w_up"][l, e].rearrange("(k p) f -> p k f", p=P)
                                 ).then_inc(s[f"wu_in{slot}"], 16)

                def down_in(e, slot):
                    sp.wait_ge(s["dn_mm"], BASE + NE * l + e + 1)
                    settle(sp, s["sp_passed"])
                    sp.dma_start(wd[slot], a["w_down"][l, e].rearrange("(k p) f -> p k f", p=P)
                                 ).then_inc(s[f"wd_in{slot}"], 16)

                sp.wait_ge(s["small_out"], BASE + 16 * 7 * (l + 1))
                settle(sp, s["sp_passed"])
                sp.wait_ge(s["gate_staged"], BASE + NT * (l + 1))
                settle(sp, s["sp_passed"])
                res_in(8, 0, NS, NT * l + 7)
                gate_up_in(0, 0)
                x1_out(6, 0, P)
                x1_out(7, 1, P)
                x1_out(8, 0, NS)
                sp.wait_ge(s["rt_mm"], BASE + NT * (l + 1))
                settle(sp, s["sp_passed"])
                sp.wait_ge(s["x1_out0"], BASE + 16 * 5 * (l + 1))
                settle(sp, s["sp_passed"])
                sp.wait_ge(s["x1_out1"], BASE + 16 * 4 * (l + 1))
                settle(sp, s["sp_passed"])
                down_in(0, 0)
                gate_up_in(1, 1)
                down_in(1, 1)
                settle(sp, s["sp_passed"])
                with sp.Fori(0, NE // 2 - 1) as i:
                    for slot in range(2):
                        gate_up_in(2 * i + slot + 2, slot)
                        down_in(2 * i + slot + 2, slot)

                sp.wait_ge(s["idx_ready"], BASE + l + 1)
                settle(sp, s["sp_passed"])
                with sp.If(sp.value_load(over[0:1, OVER:OVER + 1], min_val=0, max_val=OVER) > 0):
                    sp.wait_ge(s["dn_mm"], BASE + NE * (l + 1) + 2)
                    settle(sp, s["sp_passed"])
                    with sp.Fori(0, OVER) as o:
                        sp.wait_ge(s["ov_dn"], BASE + OVER * l + o)
                        settle(sp, s["sp_passed"])
                        e = sp.value_load(over[0:1, ds(o, 1)], min_val=0, max_val=NE - 1)
                        for dst, w in ((wg[0], "w_gate"), (wu[0], "w_up"), (wd[0], "w_down")):
                            sp.dma_start(dst, a[w][l, e].rearrange("(k p) f -> p k f", p=P)
                                         ).then_inc(s["ov_w"], 16)
                with sp.Else():
                    sp.sem_inc(s["ov_w"], 48 * OVER)
                sp.wait_ge(s["ov_out"], BASE + OVER * (l + 1))
                settle(sp, s["sp_passed"])

                def l2(t, slot, rows, after):
                    sp.wait_ge(s["l2_add"], BASE + after)
                    settle(sp, s["sp_passed"])
                    for n, src in enumerate((a["ytok"][0], a["ytok"][1], a["xs1"])):
                        sp.dma_start(l2in[0:rows, slot, n * DM:(n + 1) * DM], src[ds(t * P, rows), :]
                                     ).then_inc(s[f"l2_in{slot}"], 16)

                def x2_out(t, slot, rows):
                    sp.wait_ge(s["x2_ready"], BASE + NT * l + t + 1)
                    settle(sp, s["sp_passed"])
                    sp.dma_start(a["y_all"][l + 1, ds(t * P, rows), :], x2[0:rows, slot]
                                 ).then_inc(s[f"x2_out{slot}"], 16)

                sp.wait_ge(s["sc_out0"], 16 * (NE // 2) * (l + 1))
                sp.wait_ge(s["sc_out1"], 16 * (NE // 2) * (l + 1))
                l2(0, 0, P, NT * l)
                l2(1, 1, P, NT * l)
                l2(2, 0, P, NT * l + 1)
                settle(sp, s["sp_passed"])
                with sp.Fori(0, 2) as i:
                    for slot in range(2):
                        l2(2 * i + slot + 3, 1 - slot, P, NT * l + 2 * i + slot + 2)
                        x2_out(2 * i + slot, slot, P)
                l2(7, 1, P, NT * l + 6)
                x2_out(4, 0, P)
                l2(8, 0, NS, NT * l + 7)
                x2_out(5, 1, P)
                x2_out(6, 0, P)
                x2_out(7, 1, P)
                with sp.If(l < DEPTH - 1):
                    for slot in range(3):
                        w_tile((l + 1) % DEPTH * NTILE + slot, slot)
                x2_out(8, 0, NS)
                sp.wait_ge(s["x2_out0"], BASE + 16 * 5 * (l + 1))
                settle(sp, s["sp_passed"])
                sp.wait_ge(s["x2_out1"], BASE + 16 * 4 * (l + 1))
                settle(sp, s["sp_passed"])

        @block.tensor
        def _(pe):
            raise_to_base(pe, "tensor")
            mm = nc.tensor.matmul
            tr = nc.tensor.transpose
            pe.sem_inc(s["xt_mm"], 2)
            pe.sem_inc(s["proj_mm"], 6)
            pe.sem_inc(s["wo_mm"], 2)
            pe.sem_inc(s["gu_mm"], 4)
            pe.sem_inc(s["dn_mm"], 2)
            pe.sem_inc(s["xg_mm"], 2)
            pe.wait_ge(s["ident_in"], BASE + 16)

            def x_transposed(g, slot, rows):
                pe.wait_ge(s["xt_a"], BASE + g + 1)
                pe.wait_ge(s["xt_d"], BASE + g + 1)
                if rows < P:
                    settle(pe, s["pe_passed"])
                for k in range(KD):
                    last = tr(ps[:, 2 * slot + k // 4, (k % 4) * P:(k % 4) * P + rows],
                              x2[0:rows, slot, k * P:(k + 1) * P], ident[0:rows, 0:rows])
                last.then_inc(s["xt_mm"], 1)

            settle(pe, s["pe_passed"])
            with pe.Fori(0, 4) as i:
                for slot in range(2):
                    pe.wait_ge(s[f"xin{slot}"], BASE + 16 * (i + 1))
                    x_transposed(2 * i + slot, slot, P)
            pe.wait_ge(s["xin0"], BASE + 16 * 5)
            x_transposed(8, 0, NS)

            settle(pe, s["pe_passed"])
            with pe.Fori(0, DEPTH) as l:
                pe.wait_ge(s["xt_a"], BASE + NT * (l + 1) + 2)
                pe.wait_ge(s["xt_d"], BASE + NT * (l + 1) + 2)

                def project(c, slot, half, turn):
                    pe.wait_ge(s[f"w_in{slot}"], BASE + 16 * (6 * l + turn + 1))
                    for ch in range(NCH):
                        pe.wait_ge(s["act_ev"], BASE + (l * NTILE + c) * NCH + ch + 1)
                        for k in range(KD):
                            last = mm(ps[:, 3 * half + ch, 0:CH], wring[:, slot, k * P:(k + 1) * P],
                                      xT[:, k, ch * CH:(ch + 1) * CH], start=(k == 0), stop=(k == KD - 1))
                        last.then_inc(s["proj_mm"], 1)

                def rotate(r):
                    for ch in range(NCH):
                        i = NCH * r + ch
                        pe.wait_ge(s["act_ev"], BASE + (l * NTILE + r) * NCH + ch + 1 + 6)
                        pe.wait_ge(s["rot_used"], BASE + 15 * l + max(i - 1, 0))
                        mm(ps[:, 6 + i % 2, 0:CH], rotm[:], ztmp[:, r % 2, ch * CH:(ch + 1) * CH],
                           start=True, stop=True).then_inc(s["rot_mm"], 1)

                for c in range(6):
                    project(c, c % 3, c % 2, c // 3)
                    if c == 0:
                        pe.wait_ge(s["const_in"], BASE + 16 * N_CONST)
                        pe.wait_ge(s["init"], BASE + 6)
                    if c:
                        rotate(c - 1)
                settle(pe, s["pe_passed"])
                with pe.Fori(0, CG // 2) as i:
                    for n in range(6):
                        project(6 + 6 * i + n, n % 3, n % 2, 2 + 2 * i + n // 3)

                pe.wait_ge(s["wo_in"], BASE + 16 * (l + 1))
                pe.wait_ge(s["lnp_in"], BASE + 16 * (l + 1))

                def values_transposed(b):
                    pe.wait_ge(s["stage_done"], BASE + NB * l + b + 1)
                    pe.wait_ge(s["o_norm"], BASE + NB * l + b)
                    tr(ps[:, 4, 0:P], vs, ident[:]).then_inc(s["v_t"], 1)
                    pe.wait_ge(s["pt_ev"], BASE + 2 * (NB * l + b))

                def scores(b, slot, h):
                    for j in range(QPK):
                        last = mm(ps[:, 2 * h + j // 2, (j % 2) * 256:(j % 2) * 256 + 256],
                                  qs[h * HD:(h + 1) * HD, slot, j], kwin[h * HD:(h + 1) * HD, :],
                                  start=True, stop=True)
                    last.then_inc(s["s_mm"], 1)

                def weighted_values(b, slot):
                    n = NB * l + b
                    for h in range(NKV):
                        pe.wait_ge(s["p_ready"], BASE + 2 * n + h + 1)
                        for j in range(QPK):
                            for w in range(2):
                                last = tr(ps[:, 2 * h + j // 2, (j % 2) * 256 + w * P:(j % 2) * 256 + (w + 1) * P],
                                          sS[:, h, j, w * P:(w + 1) * P], ident[:])
                        last.then_inc(s["pt_mm"], 1)
                    pe.wait_ge(s["v_ev"], BASE + n + 1)
                    for h in range(NKV):
                        pe.wait_ge(s["pt_ev"], BASE + 2 * n + h + 1)
                        for j in range(QPK):
                            c = (QPK * h + j) * HD
                            for w in range(2):
                                last = mm(ps[:, 4, c:c + HD], pT[:, h, j, w], vnat[:, w, h * HD:(h + 1) * HD],
                                          start=(w == 0), stop=(w == 1))
                    last.then_inc(s["pv_mm"], 1)

                def o_transposed(b, routed):
                    n = NB * l + b
                    pe.wait_ge(s["o_norm"], BASE + n + 1)
                    pe.wait_ge(s["lg_ev"], BASE + NT * l + routed)
                    for j in range(4):
                        last = tr(ps[:, 5, j * P:(j + 1) * P], oS[:, j * P:(j + 1) * P], ident[:])
                    last.then_inc(s["ot_mm"], 1)

                def out_project(b, slot, rows, between=()):
                    m = NT * l + b
                    between = dict(between)
                    if rows == P:
                        pe.wait_ge(s["ot_ev"], BASE + NB * l + b + 1)
                    else:
                        pe.wait_ge(s["smp_mix"], BASE + l + 1)
                    pe.wait_ge(s["gate_staged"], BASE + m + 1)
                    if rows == P:
                        pe.wait_ge(s["x1t_a"], BASE + m)
                        pe.wait_ge(s["x1t_d"], BASE + m)
                    else:
                        pe.wait_ge(s["x1t_a"], BASE + m - 1)
                        pe.wait_ge(s["x1t_d"], BASE + m - 1)
                        pe.wait_ge(s["ln_add"], BASE + m)
                    for n in range(2):
                        for k in range(KD):
                            if n * KD + k in between:
                                between[n * KD + k]()
                            last = mm(ps[0:rows, 6 + n, :], mixT[:, slot, k, 0:rows], wo[:, k, n * 512:(n + 1) * 512],
                                      start=(k == 0), stop=(k == KD - 1))
                    last.then_inc(s["wo_mm"], 1)

                def x1_transposed(b, slot, rows):
                    m = NT * l + b
                    pe.wait_ge(s["x1_ready"], BASE + m + 1)
                    if rows < P:
                        settle(pe, s["pe_passed"])
                    for k in range(KD):
                        last = tr(ps[:, 6 + k // 4, (k % 4) * P:(k % 4) * P + rows],
                                  x1[0:rows, slot, k * P:(k + 1) * P], ident[0:rows, 0:rows])
                    last.then_inc(s["x1t_mm"], 1)

                def route(b, rows):
                    m = NT * l + b
                    pe.wait_ge(s["x1t_a"], BASE + m + 1)
                    pe.wait_ge(s["x1t_d"], BASE + m + 1)
                    settle(pe, s["pe_passed"])
                    for k in range(KD):
                        last = mm(ps[0:rows, 5, 0:NR], x1T[:, k, 0:rows], wr_l[k], start=(k == 0), stop=(k == KD - 1))
                    last.then_inc(s["rt_mm"], 1)

                wr_l = [wr[:, ds(l, 1), k, :].rearrange("p a n -> p (a n)") for k in range(KD)]
                values_transposed(0)
                scores(0, 0, 0)
                scores(0, 0, 1)
                weighted_values(0, 0)
                o_transposed(0, 0)
                values_transposed(1)
                scores(1, 1, 0)
                scores(1, 1, 1)
                out_project(0, 0, P)
                weighted_values(1, 1)
                o_transposed(1, 0)
                settle(pe, s["pe_passed"])
                with pe.Fori(0, 3) as i:
                    for slot in range(2):
                        b = 2 * i + slot + 2
                        values_transposed(b)
                        scores(b, slot, 0)
                        x1_transposed(b - 2, slot, P)
                        scores(b, slot, 1)
                        out_project(b - 1, 1 - slot, P)
                        route(b - 2, P)
                        weighted_values(b, slot)
                        o_transposed(b, b - 1)

                pe.wait_ge(s["smp_q"], BASE + l + 1)
                pe.wait_ge(s["smp_in"], BASE + 32 * (l + 1))
                pe.wait_ge(s["pt_ev"], BASE + 2 * NB * (l + 1))
                for b in range(NS):
                    last = mm(ps[0:64, 0, 0:P + 1], qz[:, b * 64:(b + 1) * 64], kTs[:, b, :],
                              start=(b == 0), stop=(b == NS - 1))
                last.then_inc(s["smp_s"], 1)
                x1_transposed(6, 0, P)

                def sample_probs():
                    pe.wait_ge(s["smp_p"], BASE + l + 1)
                    settle(pe, s["pe_passed"])
                    tr(ps[:, 1, 0:64], ssn[:, 0:P], ident[0:64, 0:64])
                    mm(ps[0:NS, 2, 0:64], sel8[:], diag, start=True, stop=True)
                    tr(ps[0:NS, 3, 0:P], zT[:, 5, SEQ:T], ident[:]).then_inc(s["smp_t"], 1)

                def sample_values():
                    pe.wait_ge(s["smp_pt"], BASE + l + 1)
                    for b in range(NS):
                        mm(ps[0:64, 4, 0:P], ptz[:, b * 64:(b + 1) * 64], vS[:, b, :], start=(b == 0), stop=False)
                    mm(ps[0:64, 4, 0:P], pnew, vnew, start=False, stop=True).then_inc(s["smp_o"], 1)

                def sample_turned():
                    pe.wait_ge(s["smp_sel"], BASE + l + 1)
                    settle(pe, s["pe_passed"])
                    tr(ps[0:64, 1, 0:64], osel, ident[0:64, 0:64]).then_inc(s["smp_ot"], 1)

                out_project(7, 1, P, ((6, sample_probs), (9, sample_values), (13, sample_turned)))
                route(6, P)
                out_project(8, 0, NS)
                pe.wait_ge(s["ln_add"], BASE + NT * (l + 1))
                x1_transposed(7, 1, P)
                route(7, P)
                x1_transposed(8, 0, NS)
                route(8, NS)

                pe.wait_ge(s["rk_m"], BASE + l + 1)
                mm(ps[:, 4, 0:NT * NE], upper[:], rt[4].rearrange("p t e -> p (t e)"), start=True, stop=False)
                mm(ps[:, 4, 0:NT * NE], ones[:], rt[5].rearrange("p t e -> p (t e)"), start=False, stop=True)
                mm(ps[:, 5, 0:NE], ones[:], rt[6][:, 0, :], start=True, stop=True).then_inc(s["rk_c"], 1)
                for i in range(2 * NT):
                    if i % NT == 0:
                        pe.wait_ge(s["rk_r"], BASE + 2 * l + i // NT + 1)
                    last = mm(ps[:, 0, 0:3 * NBLK], slot_of[:, i], block_of[:, i],
                              start=(i == 0), stop=(i == 2 * NT - 1))
                last.then_inc(s["rk_inv"], 1)

                def gathered(e, slot, turn):
                    n = NE * l + e
                    pe.wait_ge(s[f"xg_in{slot}"], 16 * (NE // 2 * l + turn + 1))
                    pe.wait_ge(s["xg_a"], BASE + n)
                    pe.wait_ge(s["xg_d"], BASE + n)
                    for k in range(KD):
                        last = tr(ps[:, k // 4, (k % 4) * P:(k % 4 + 1) * P], xg[:, slot, k * P:(k + 1) * P], ident[:])
                    last.then_inc(s["xg_mm"], 1)

                def gate_up(e, slot, turn):
                    n = NE * l + e
                    pe.wait_ge(s["xg_a"], BASE + n + 1)
                    pe.wait_ge(s["xg_d"], BASE + n + 1)
                    pe.wait_ge(s[f"wg_in{slot}"], BASE + 16 * (NE // 2 * l + turn + 1))
                    pe.wait_ge(s[f"wu_in{slot}"], BASE + 16 * (NE // 2 * l + turn + 1))
                    pe.wait_ge(s["h_ready"], BASE + 2 * n + 2)
                    for f in range(FD):
                        bank, c = 2 + 2 * slot + f // 2, (f % 2) * P
                        for w, at_c in ((wg, c), (wu, c + 2 * P)):
                            for k in range(KD):
                                last = mm(ps[:, bank, at_c:at_c + P], w[slot][:, k, f * P:(f + 1) * P],
                                          xgT[:, slot, k], start=(k == 0), stop=(k == KD - 1))
                        if f % 2:
                            last.then_inc(s["gu_mm"], 1)

                def down(e, slot, turn):
                    n = NE * l + e
                    pe.wait_ge(s["h_ready"], BASE + 2 * n + 2 + 4)
                    pe.wait_ge(s[f"wd_in{slot}"], BASE + 16 * (NE // 2 * l + turn + 1))
                    pe.wait_ge(s["y_a"], BASE + n)
                    pe.wait_ge(s["y_d"], BASE + n)
                    for h in range(2):
                        for f in range(FD):
                            last = mm(ps[:, 6 + h, :], hT[:, slot, f], wd[slot][:, f, h * 512:(h + 1) * 512],
                                      start=(f == 0), stop=(f == FD - 1))
                    last.then_inc(s["dn_mm"], 1)

                gathered(0, 0, 0)
                settle(pe, s["pe_passed"])
                with pe.Fori(0, NE // 2 - 1) as i:
                    gate_up(2 * i, 0, i)
                    gathered(2 * i + 1, 1, i)
                    down(2 * i, 0, i)
                    gate_up(2 * i + 1, 1, i)
                    gathered(2 * i + 2, 0, i + 1)
                    down(2 * i + 1, 1, i)
                i = NE // 2 - 1
                gate_up(2 * i, 0, i)
                gathered(2 * i + 1, 1, i)
                down(2 * i, 0, i)
                gate_up(2 * i + 1, 1, i)
                down(2 * i + 1, 1, i)

                settle(pe, s["pe_passed"])
                with pe.If(pe.value_load(over[0:1, OVER:OVER + 1], min_val=0, max_val=OVER) > 0):
                    pe.wait_ge(s["y_a"], BASE + NE * (l + 1))
                    pe.wait_ge(s["y_d"], BASE + NE * (l + 1))
                    settle(pe, s["pe_passed"])
                    with pe.Fori(0, OVER) as o:
                        n = OVER * l + o
                        pe.wait_ge(s["ov_xin"], BASE + n + 1)
                        for k in range(KD):
                            last = tr(ps[:, k // 4, (k % 4) * P:(k % 4 + 1) * P], xg[:, 0, k * P:(k + 1) * P], ident[:])
                        last.then_inc(s["ov_xt"], 1)
                        pe.wait_ge(s["ov_xa"], BASE + n + 1)
                        pe.wait_ge(s["ov_w"], BASE + 48 * (n + 1))
                        for f in range(FD):
                            for w, bank in ((wg, 2), (wu, 4)):
                                for k in range(KD):
                                    last = mm(ps[:, bank, f * P:(f + 1) * P], w[0][:, k, f * P:(f + 1) * P],
                                              xgT[:, 0, k], start=(k == 0), stop=(k == KD - 1))
                        last.then_inc(s["ov_gu"], 1)
                        pe.wait_ge(s["ov_h"], BASE + n + 1)
                        for h in range(2):
                            for f in range(FD):
                                last = mm(ps[:, 6 + h, :], hT[:, 0, f], wd[0][:, f, h * 512:(h + 1) * 512],
                                          start=(f == 0), stop=(f == FD - 1))
                        last.then_inc(s["ov_dn"], 1)
                with pe.Else():
                    pe.sem_inc(s["ov_xt"], OVER)
                    pe.sem_inc(s["ov_gu"], OVER)
                    pe.sem_inc(s["ov_dn"], OVER)

                settle(pe, s["pe_passed"])
                with pe.Fori(0, 4) as i:
                    for slot in range(2):
                        pe.wait_ge(s["x2_ready"], BASE + NT * l + 2 * i + slot + 1)
                        x_transposed(NT * (l + 1) + 2 * i + slot, slot, P)
                pe.wait_ge(s["x2_ready"], BASE + NT * l + 9)
                x_transposed(NT * (l + 1) + 8, 0, NS)

        @block.scalar
        def _(act):
            raise_to_base(act, "scalar")
            act.sem_inc(s["xt_a"], 2)
            act.sem_inc(s["act_ev"], 6)

            def xt_evict(g, slot, col, rows):
                act.wait_ge(s["xt_mm"], BASE + g + 3)
                nc.scalar.copy(xT[:, 0:4, ds(col, rows)],
                               ps[:, 2 * slot, :].rearrange("p (k t) -> p k t", k=4)[:, :, 0:rows]
                               ).then_inc(s["xt_a"], 1)

            def xt_tiles(g0):
                with act.Fori(0, 4) as i:
                    for slot in range(2):
                        xt_evict(g0 + 2 * i + slot, slot, (2 * i + slot) * P, P)
                xt_evict(g0 + 8, 0, SEQ, NS)

            xt_tiles(0)

            with act.Fori(0, DEPTH) as l:
                def evict(c, half, dst):
                    for ch in range(NCH):
                        n = (l * NTILE + c) * NCH + ch
                        act.wait_ge(s["proj_mm"], BASE + n + 1 + 6)
                        nc.scalar.copy(dst[:, ch * CH:(ch + 1) * CH], ps[:, 3 * half + ch, 0:CH]
                                       ).then_inc(s["act_ev"], 1)

                for c in range(5):
                    act.wait_ge(s["rot_mm"], BASE + 15 * l + max(c - 1, 0) * NCH)
                    act.wait_ge(s["cos_done"], BASE + 15 * l + max(c - 1, 0) * NCH)
                    evict(c, c % 2, ztmp[:, c % 2])
                evict(5, 1, zT[:, 5])
                with act.Fori(0, CG // 2) as i:
                    for n in range(6):
                        if n % 3 == 0:
                            act.wait_ge(s["conv_done"], BASE + CG * l + 2 * i + n // 3)
                        evict(6 + 6 * i + n, n % 2, (cbuf, hbuf, bbuf)[n % 3])

                def softmax(b):
                    n = NB * l + b
                    for h in range(NKV):
                        act.wait_ge(s["sm_ready"], BASE + 2 * n + h + 1)
                        for j in range(QPK):
                            nc.scalar.activation(sS[:, h, j], sS[:, h, j], ACT.Exp, bias=sm[:, h, 1, j:j + 1],
                                                 accum_out=sm[:, h, 3, j:j + 1])
                        nc.scalar.activation(sm[:, h, 4], sm[:, h, 2], ACT.Exp).then_inc(s["p_ready"], 1)

                def pt_evict(b):
                    n = NB * l + b
                    act.wait_ge(s["pv_mm"], BASE + n)
                    for h in range(NKV):
                        act.wait_ge(s["pt_mm"], BASE + 2 * n + h + 1)
                        nc.scalar.copy(pT[:, h].rearrange("p j w k -> p (j w k)"),
                                       ps[:, 2 * h:2 * h + 2, :].rearrange("p a b -> p (a b)")
                                       ).then_inc(s["pt_ev"], 1)

                def normed(b, rows):
                    m = NT * l + b
                    act.wait_ge(s["ln_rstd"], BASE + m + 1)
                    nc.scalar.activation(t1[0:rows], t1[0:rows], ACT.Identity, bias=rstd[0:rows, 0, 1:2],
                                         scale=rstd[0:rows, 0, 0:1]).then_inc(s["ln_hat"], 1)

                def x1t_evict(b, rows):
                    m = NT * l + b
                    act.wait_ge(s["x1t_mm"], BASE + m + 1)
                    act.wait_ge(s["rt_mm"], BASE + m)
                    nc.scalar.copy(x1T[:, 0:4, 0:rows],
                                   ps[:, 6, :].rearrange("p (k t) -> p k t", k=4)[:, :, 0:rows]
                                   ).then_inc(s["x1t_a"], 1)

                def ot_evict(b, slot):
                    act.wait_ge(s["ot_mm"], BASE + NB * l + b + 1)
                    act.wait_ge(s["wo_mm"], BASE + NT * l + b + 1)
                    nc.scalar.copy(mixT[:, slot, 0:4].rearrange("p k t -> p (k t)"), ps[:, 5, :]
                                   ).then_inc(s["ot_ev"], 1)

                softmax(0)
                pt_evict(0)
                ot_evict(0, 0)
                softmax(1)
                pt_evict(1)
                normed(0, P)
                ot_evict(1, 1)
                with act.Fori(0, 3) as i:
                    for slot in range(2):
                        b = 2 * i + slot + 2
                        x1t_evict(b - 2, P)
                        softmax(b)
                        pt_evict(b)
                        normed(b - 1, P)
                        ot_evict(b, slot)
                x1t_evict(6, P)

                act.wait_ge(s["smp_max"], BASE + l + 1)
                nc.scalar.activation(ss, ss, ACT.Exp, bias=smp[:, 1:2], accum_out=smp[:, 3:4])
                nc.scalar.activation(smp[:, 4:5], smp[:, 2:3], ACT.Exp).then_inc(s["smp_n"], 1)
                normed(7, P)
                x1t_evict(7, P)
                normed(8, NS)
                x1t_evict(8, NS)

                act.wait_ge(s["rk_soft"], BASE + l + 1)
                nc.scalar.activation(rt[7][:, :, 0:NG], rt[7][:, :, 0:NG], ACT.Exp)
                nc.scalar.activation(rt[7][:, :, 8:9], rt[7][:, :, 8:9], ACT.Exp).then_inc(s["rk_exp"], 1)

                def xg_evict(e, slot):
                    n = NE * l + e
                    act.wait_ge(s["xg_mm"], BASE + n + 3)
                    act.wait_ge(s["gu_mm"], BASE + 2 * n + 2)
                    nc.scalar.copy(xgT[:, slot, 0:4].rearrange("p k t -> p (k t)"), ps[:, 0, :]
                                   ).then_inc(s["xg_a"], 1)

                def silu(e, slot):
                    n = NE * l + e
                    for q in range(2):
                        act.wait_ge(s["gu_mm"], BASE + 2 * n + q + 1 + 4)
                        act.wait_ge(s["h_ready"], BASE + 2 * n + q - 1 + 4)
                        nc.scalar.activation(sg[:, 2 * q:2 * q + 2].rearrange("p f t -> p (f t)"),
                                             ps[:, 2 + 2 * slot + q, 0:2 * P], ACT.Silu
                                             ).then_inc(s["silu"], 1)

                def y_evict(e, slot, turn, col):
                    n = NE * l + e
                    act.wait_ge(s["dn_mm"], BASE + n + 3)
                    act.wait_ge(s["ys_free"], BASE + n + 1)
                    nc.scalar.activation(ys[:, slot, 0:512], ps[:, 6, :], ACT.Copy, scale=col).then_inc(s["y_a"], 1)

                def gate_of(e):
                    return inv[:, 2, ds(e, 1)]

                xg_evict(0, 0)
                with act.Fori(0, NE // 2 - 1) as i:
                    silu(2 * i, 0)
                    xg_evict(2 * i + 1, 1)
                    y_evict(2 * i, 0, i, gate_of(2 * i))
                    silu(2 * i + 1, 1)
                    xg_evict(2 * i + 2, 0)
                    y_evict(2 * i + 1, 1, i, gate_of(2 * i + 1))
                i = NE // 2 - 1
                silu(2 * i, 0)
                xg_evict(2 * i + 1, 1)
                y_evict(2 * i, 0, i, gate_of(2 * i))
                silu(2 * i + 1, 1)
                y_evict(2 * i + 1, 1, i, gate_of(2 * i + 1))

                with act.If(act.value_load(over[0:1, OVER:OVER + 1], min_val=0, max_val=OVER) > 0):
                    with act.Fori(0, OVER) as o:
                        n = OVER * l + o
                        act.wait_ge(s["ov_xt"], BASE + n + 1)
                        nc.scalar.copy(xgT[:, 0].rearrange("p k t -> p (k t)"),
                                       ps[:, 0:2, :].rearrange("p a b -> p (a b)")).then_inc(s["ov_xa"], 1)
                        act.wait_ge(s["ov_gu"], BASE + n + 1)
                        nc.scalar.activation(sg.rearrange("p f t -> p (f t)"), ps[:, 2, :], ACT.Silu
                                             ).then_inc(s["ov_silu"], 1)
                with act.Else():
                    act.sem_inc(s["ov_xa"], OVER)
                    act.sem_inc(s["ov_silu"], OVER)

                def normed2(t, slot, rows):
                    act.wait_ge(s["l2_rstd"], BASE + NT * l + t + 1)
                    nc.scalar.activation(t2_of(t, rows), t2_of(t, rows), ACT.Identity,
                                         bias=rstd[0:rows, slot, 1:2], scale=rstd[0:rows, slot, 0:1]
                                         ).then_inc(s["l2_hat"], 1)

                normed2(0, 0, P)
                normed2(1, 1, P)
                with act.Fori(0, 3) as i:
                    for slot in range(2):
                        normed2(2 * i + slot + 2, slot, P)
                        xt_evict(NT * (l + 1) + 2 * i + slot, slot, (2 * i + slot) * P, P)
                normed2(8, 0, NS)
                xt_evict(NT * (l + 1) + 6, 0, 6 * P, P)
                xt_evict(NT * (l + 1) + 7, 1, 7 * P, P)
                xt_evict(NT * (l + 1) + 8, 0, SEQ, NS)

        @block.vector
        def _(dve):
            raise_to_base(dve, "vector")
            v = nc.vector
            step = Steps(dve, s["dve_step"])
            dve.sem_inc(s["xt_d"], 2)
            dve.sem_inc(s["h_ready"], 4)
            v.memset(ones[:], 1.0).then_inc(s["init"], 1)
            v.memset(mhalf[:], -0.5).then_inc(s["init"], 1)
            v.memset(kwin[:], 0.0).then_inc(s["init"], 1)
            v.memset(vnat[:], 0.0).then_inc(s["init"], 1)
            v.memset(logits[:], 0.0).then_inc(s["init"], 1)
            v.memset(over_f[:], 0.0).then_inc(s["init"], 1)

            def xt_evict(g, slot, col, rows):
                dve.wait_ge(s["xt_mm"], BASE + g + 3)
                v.tensor_copy(xT[:, 4:8, ds(col, rows)],
                              ps[:, 2 * slot + 1, :].rearrange("p (k t) -> p k t", k=4)[:, :, 0:rows]
                              ).then_inc(s["xt_d"], 1)

            settle(dve, s["dve_passed"])
            with dve.Fori(0, 4) as i:
                for slot in range(2):
                    xt_evict(2 * i + slot, slot, (2 * i + slot) * P, P)
            xt_evict(8, 0, SEQ, NS)
            dve.wait_ge(s["init"], BASE + 6)
            dve.wait_ge(s["const_in"], BASE + 16 * N_CONST)
            settle(dve, s["dve_passed"])

            def moments(t, slot, rows, done):
                for h in range(2):
                    step.mark(v.bn_stats(stat[0:rows, 6 * h:6 * h + 6], t[:, h * 512:(h + 1) * 512]))
                step.wait()
                settle(dve, s["dve_passed"])
                v.bn_aggr(mv[0:rows, slot], stat[0:rows]).then_inc(done, 1)

            with step.loop(DEPTH, STEPS_LAYER) as l:
                for r in range(5):
                    for ch in range(NCH):
                        i = NCH * r + ch
                        cols = slice(ch * CH, (ch + 1) * CH)
                        dve.wait_ge(s["rot_mm"], BASE + 15 * l + i + 1)
                        v.tensor_tensor(rot[:, i % 2], ps[:, 6 + i % 2, 0:CH], sinT[:, cols], ALU.mult
                                        ).then_inc(s["rot_used"], 1)
                        dve.wait_ge(s["rot_used"], BASE + 15 * l + i + 1)
                        dve.wait_ge(s["cos_done"], BASE + 15 * l + i + 1)
                        v.tensor_tensor(zT[:, r, cols], zT[:, r, cols], rot[:, i % 2], ALU.add
                                        ).then_inc(s["rope_done"], 1)

                dve.wait_ge(s["state_set"], BASE + l + 1)
                step.link(v.memset(u[:, 0:2], 0.0))
                settle(dve, s["dve_passed"])
                with step.loop(CG, 9) as g:
                    dve.wait_ge(s["act_ev"], BASE + (l * NTILE + 6 + 3 * g + 3) * NCH + 6)
                    cw = [convw[:, ds(l, 1), ds(g, 1), j:j + 1].rearrange("p a b c -> p (a b c)") for j in range(3)]
                    sug = su[:, ds(g * NS, NS), :]
                    step.mark(v.tensor_tensor(u[:, 2:SEQ + 2], cbuf[:, 0:SEQ], hbuf[:, 0:SEQ], ALU.mult))
                    step.link(v.tensor_tensor(sug[:, :, 2], cbuf[:, SEQ:T], hbuf[:, SEQ:T], ALU.mult))
                    step.mark(v.tensor_copy(upo[:, ds(g, 1), :].rearrange("p a b -> p (a b)"), u[:, SEQ:SEQ + 2]))
                    accs = hbuf[:, SEQ:T]
                    step.mark(v.tensor_scalar(acc, u[:, 0:SEQ], cw[0], None, ALU.mult))
                    step.link(v.tensor_scalar(accs, sug[:, :, 0], cw[0], None, ALU.mult))
                    step.mark(v.scalar_tensor_tensor(acc, u[:, 1:SEQ + 1], cw[1], acc, ALU.mult, ALU.add))
                    step.link(v.scalar_tensor_tensor(accs, sug[:, :, 1], cw[1], accs, ALU.mult, ALU.add))
                    step.mark(v.scalar_tensor_tensor(acc, u[:, 2:SEQ + 2], cw[2], acc, ALU.mult, ALU.add))
                    step.link(v.scalar_tensor_tensor(accs, sug[:, :, 2], cw[2], accs, ALU.mult, ALU.add))
                    gTg = gT[:, ds(g, 1), :].rearrange("p a b -> p (a b)")
                    v.tensor_tensor(gTg[:, 0:SEQ], acc, bbuf[:, 0:SEQ], ALU.mult)
                    v.tensor_tensor(gTg[:, SEQ:T], accs, bbuf[:, SEQ:T], ALU.mult).then_inc(s["conv_done"], 1)

                def values(b, slot):
                    n = NB * l + b
                    dve.wait_ge(s["v_t"], BASE + n + 1)
                    dve.wait_ge(s["pv_mm"], BASE + n)
                    v.tensor_copy(vnat[:, slot], ps[:, 4, 0:P]).then_inc(s["v_ev"], 1)

                def max_of(b, mask):
                    n = NB * l + b
                    for h in range(NKV):
                        dve.wait_ge(s["s_mm"], BASE + 2 * n + h + 1)
                        step.link(v.scalar_tensor_tensor(
                            sS[:, h], ps[:, 2 * h:2 * h + 2, :].rearrange("p a (c k) -> p (a c) k", c=2), HD ** -0.5,
                            masks[:, mask:mask + 1, :].broadcast_to([P, QPK, 2 * P]), ALU.mult, ALU.add))
                        step.link(v.tensor_reduce(sm[:, h, 0], sS[:, h], AX.X, ALU.max))
                        sk = sinks[:, ds(l * NH + h * QPK, QPK)]
                        step.link(v.tensor_tensor(sm[:, h, 0], sm[:, h, 0], sk, ALU.max))
                        step.mark(v.tensor_scalar(sm[:, h, 1], sm[:, h, 0], -1.0, None, ALU.mult))
                        step.link(v.tensor_tensor(sm[:, h, 2], sk, sm[:, h, 0], ALU.subtract))
                        dve.sem_inc(s["sm_ready"], 1)

                def residual(b, slot, rows, turn):
                    m = NT * l + b
                    dve.wait_ge(s["wo_mm"], BASE + m + 3)
                    dve.wait_ge(s["x1_ready"], BASE + m)
                    dve.wait_ge(s[f"xr_in{slot}"], BASE + 16 * ((5 - slot) * l + turn + 1))
                    v.scalar_tensor_tensor(t1[0:rows], xres[0:rows, slot], ALPHA,
                                           ps[0:rows, 6:8, :].rearrange("p a b -> p (a b)"), ALU.mult, ALU.add
                                           ).then_inc(s["ln_add"], 1)
                    dve.wait_ge(s["ln_add"], BASE + m + 1)
                    moments(t1[0:rows], 0, rows, s["ln_stat"])

                def scaled(b, slot, rows, turn):
                    m = NT * l + b
                    dve.wait_ge(s["ln_hat"], BASE + m + 1)
                    v.tensor_tensor(t1[0:rows], t1[0:rows], lnp[0:rows, 0], ALU.mult).then_inc(s["ln_scaled"], 1)
                    dve.wait_ge(s["ln_scaled"], BASE + m + 1)
                    dve.wait_ge(s["x1t_mm"], BASE + m - 1)
                    dve.wait_ge(s[f"x1_out{slot}"], BASE + 16 * ((5 - slot) * l + turn))
                    v.tensor_tensor(x1[0:rows, slot], t1[0:rows], lnp[0:rows, 1], ALU.add).then_inc(s["x1_ready"], 1)

                def normalise(b):
                    n = NB * l + b
                    dve.wait_ge(s["pt_ev"], BASE + 2 * n + 2)
                    dve.wait_ge(s["ot_mm"], BASE + n)
                    step.link(v.tensor_tensor(rl[:].rearrange("p (h j) -> p h j", h=NKV), sm[:, :, 3], sm[:, :, 4], ALU.add))
                    step.link(v.reciprocal(rl[:], rl[:]))
                    dve.wait_ge(s["pv_mm"], BASE + n + 1)
                    v.tensor_tensor(oS.rearrange("p (h d) -> p h d", h=NH), ps[:, 4, :].rearrange("p (h d) -> p h d", h=NH),
                                    rl[:].unsqueeze(2).broadcast_to([P, NH, HD]), ALU.mult).then_inc(s["o_norm"], 1)

                def x1t_evict(b, rows):
                    m = NT * l + b
                    dve.wait_ge(s["x1t_mm"], BASE + m + 1)
                    dve.wait_ge(s["rt_mm"], BASE + m)
                    v.tensor_copy(x1T[:, 4:8, 0:rows],
                                  ps[:, 7, :].rearrange("p (k t) -> p k t", k=4)[:, :, 0:rows]).then_inc(s["x1t_d"], 1)

                def logit(b, rows):
                    m = NT * l + b
                    dve.wait_ge(s["rt_mm"], BASE + m + 1)
                    v.tensor_tensor(logits[0:rows, ds(b, 1), :].rearrange("p a n -> p (a n)"), ps[0:rows, 5, 0:NR],
                                    br[0:rows, ds(l, 1), :].rearrange("p a n -> p (a n)"), ALU.add
                                    ).then_inc(s["lg_ev"], 1)

                values(0, 0)
                max_of(0, 0)
                normalise(0)
                values(1, 1)
                max_of(1, 2)
                residual(0, 0, P, 0)
                normalise(1)
                scaled(0, 0, P, 0)
                settle(dve, s["dve_passed"])
                with step.loop(3, 2 * 14) as i:
                    for slot in range(2):
                        b = 2 * i + slot + 2
                        values(b, slot)
                        x1t_evict(b - 2, P)
                        max_of(b, 1 + slot)
                        residual(b - 1, 1 - slot, P, i + slot)
                        logit(b - 2, P)
                        normalise(b)
                        scaled(b - 1, 1 - slot, P, i + slot)

                dve.wait_ge(s["smp_s"], BASE + l + 1)
                sk = sinkc[:, ds(l, 1)]
                step.link(v.tensor_scalar(ss, ps[0:64, 0, 0:P + 1], HD ** -0.5, None, ALU.mult))
                step.link(v.tensor_reduce(smp[:, 0:1], ss, AX.X, ALU.max))
                step.link(v.tensor_tensor(smp[:, 0:1], smp[:, 0:1], sk, ALU.max))
                step.mark(v.tensor_scalar(smp[:, 1:2], smp[:, 0:1], -1.0, None, ALU.mult))
                v.tensor_tensor(smp[:, 2:3], sk, smp[:, 0:1], ALU.subtract).then_inc(s["smp_max"], 1)
                x1t_evict(6, P)
                dve.wait_ge(s["smp_n"], BASE + l + 1)
                step.link(v.tensor_tensor(smp[:, 5:6], smp[:, 3:4], smp[:, 4:5], ALU.add))
                step.link(v.reciprocal(smp[:, 5:6], smp[:, 5:6]))
                step.link(v.tensor_scalar(ssn, ss, smp[:, 5:6], None, ALU.mult))
                v.tensor_scalar(diag, ident[0:64, 0:64], ssn[:, P:P + 1], None, ALU.mult).then_inc(s["smp_p"], 1)
                dve.wait_ge(s["smp_t"], BASE + l + 1)
                step.mark(v.tensor_copy(ptz.rearrange("p (b x) -> p b x", b=NS)[:, :, 0:NH],
                                        ps[:, 1, 0:64].rearrange("p (b h) -> p b h", b=NS)))
                step.mark(v.tensor_copy(pnew, ps[0:NS, 2, 0:64]))
                v.tensor_copy(vnew, ps[0:NS, 3, 0:P]).then_inc(s["smp_pt"], 1)
                dve.wait_ge(s["smp_o"], BASE + l + 1)
                step.link(v.tensor_scalar(osel, ps[0:64, 4, 0:HD], half_mask[:, 0:1], None, ALU.mult))
                v.scalar_tensor_tensor(osel, ps[0:64, 4, HD:P], half_mask[:, 1:2], osel, ALU.mult, ALU.add
                                       ).then_inc(s["smp_sel"], 1)
                dve.wait_ge(s["smp_ot"], BASE + l + 1)
                dve.wait_ge(s["wo_mm"], BASE + NT * l + 9)
                oT = ps[0:64, 1, 0:64].rearrange("p (b j two) -> p two j b", b=NS, two=2)
                step.mark(v.tensor_copy(mixT[0:64, 0, 0:4, 0:NS], oT[:, 0]))
                v.tensor_copy(mixT[64:128, 0, 0:4, 0:NS], oT[:, 1]).then_inc(s["smp_mix"], 1)

                residual(7, 1, P, 3)
                logit(6, P)
                scaled(7, 1, P, 3)
                residual(8, 0, NS, 4)
                x1t_evict(7, P)
                logit(7, P)
                scaled(8, 0, NS, 4)
                x1t_evict(8, NS)
                logit(8, NS)

                def op(ins):
                    step.link(ins)

                def tt(out, in0, in1, o):
                    step.link(v.tensor_tensor(out, in0, in1, o))

                def ts(out, in0, c1, c2, o1, o2=ALU.bypass):
                    step.link(v.tensor_scalar(out, in0, c1, c2, o1, o2))

                def wide(ap, n):
                    return ap.broadcast_to([P, NT, n])

                def desc(n):
                    return rank_desc[:, NE - n:NE].unsqueeze(1).broadcast_to([P, NT, n])

                L, E, tmp, M, before, total, g7, prod, r9 = rt[0], (rt[1], rt[2]), rt[3], rt[4], rt[5], rt[6], rt[7], rt[8], rt[9]

                def first_max(values, n, top, place, onehot):
                    op(v.tensor_reduce(r9[:, :, top], values, AX.X, ALU.max))
                    tt(tmp[:, :, 0:n], values, wide(r9[:, :, top:top + 1], n), ALU.is_equal)
                    tt(tmp[:, :, 0:n], tmp[:, :, 0:n], desc(n), ALU.mult)
                    op(v.tensor_reduce(r9[:, :, place], tmp[:, :, 0:n], AX.X, ALU.max))
                    tt(onehot, desc(n), wide(r9[:, :, place:place + 1], n), ALU.is_equal)

                dve.wait_ge(s["lg_ev"], BASE + NT * (l + 1))
                dve.wait_ge(s["small_out"], BASE + 16 * 7 * (l + 1))
                gl = logits[:, :, 0:NG]
                first_max(gl, NG, 0, 1, g7[:, :, 4:8])
                tt(g7[:, :, 0:4], gl, wide(r9[:, :, 0:1], NG), ALU.subtract)
                ts(tmp[:, :, 0:4], g7[:, :, 4:8], BIG, -BIG, ALU.mult, ALU.add)
                tt(L.rearrange("p t (g e) -> p t g e", g=NG), logits[:, :, NG:NR].rearrange("p t (g e) -> p t g e", g=NG),
                   tmp[:, :, 0:4].unsqueeze(3).broadcast_to([P, NT, NG, NE_G]), ALU.add)
                first_max(L, NE, 2, 3, E[0])
                ts(prod, E[0], -BIG, None, ALU.mult)
                tt(L, L, prod, ALU.add)
                first_max(L, NE, 4, 5, E[1])
                v.tensor_tensor(g7[:, :, 8:9], r9[:, :, 4:5], r9[:, :, 2:3], ALU.subtract).then_inc(s["rk_soft"], 1)
                tt(M, E[0], E[1], ALU.add)
                tt(M, M, wide(valid[:].unsqueeze(2), NE), ALU.mult)
                step.link(v.memset(before[:, 0], 0.0))
                for t in range(NT - 1):
                    tt(before[:, t + 1], before[:, t], M[:, t], ALU.add)
                v.tensor_tensor(total[:, 0], before[:, NT - 1], M[:, NT - 1], ALU.add).then_inc(s["rk_m"], 1)
                dve.wait_ge(s["rk_exp"], BASE + l + 1)
                op(v.tensor_reduce(r9[:, :, 6], g7[:, :, 0:4], AX.X, ALU.add))
                ts(r9[:, :, 7], g7[:, :, 8], 1.0, None, ALU.add)
                tt(r9[:, :, 6], r9[:, :, 6], r9[:, :, 7], ALU.mult)
                gate = rk[:, 0]
                op(v.reciprocal(gate[:, 0:NT], r9[:, :, 6]))
                tt(gate[:, NT:2 * NT], gate[:, 0:NT], g7[:, :, 8], ALU.mult)
                dve.wait_ge(s["rk_c"], BASE + l + 1)
                ts(ovs[:, 0], ps[:, 5, 0:NE], 127.0, None, ALU.add)
                op(v.tensor_copy(rki[:, 0:NE], ovs[:, 0]))
                ts(rki[:, 0:NE], rki[:, 0:NE], 7, None, ALU.logical_shift_right)
                op(v.tensor_copy(ovs[:, 0], rki[:, 0:NE]))
                ts(ovs[:, 0], ovs[:, 0], -1.0, 0.0, ALU.add, ALU.max)
                op(v.tensor_tensor_scan(ovs[:, 1], ones[:, 0:NE], ovs[:, 0], 0.0, ALU.mult, ALU.add))
                tt(ovs[:, 2], ovs[:, 1], ovs[:, 0], ALU.subtract)
                tt(over_cmp[:], ovs[0:1, 1:2, :].broadcast_to([1, OVER, NE]),
                   iota[0:1, 0:OVER].unsqueeze(2).broadcast_to([1, OVER, NE]), ALU.is_le)
                op(v.tensor_reduce(over_f[:, 0:OVER], over_cmp[:], AX.X, ALU.add))
                ts(over_f[:, 0:OVER], over_f[:, 0:OVER], float(NE - 1), None, ALU.min)
                op(v.tensor_copy(over_f[:, OVER:OVER + 1], ovs[0:1, 1, NE - 1:NE]))
                op(v.tensor_copy(over_f[:, OVER + 1:OVER + 2], over_f[:, OVER + 2:OVER + 3]))
                op(v.tensor_copy(over[:], over_f[:]))
                op(v.scalar_tensor_tensor(over_f[:, OVER + 2:OVER + 3], over_f[:, OVER:OVER + 1], 1.0,
                                          over_f[:, OVER + 2:OVER + 3], ALU.min, ALU.add))
                rank, expert, base, hi, lo, col, low = (rk[:, n] for n in range(1, 8))
                for k in range(2):
                    c = slice(k * NT, (k + 1) * NT)
                    tt(prod, ps[:, 4, 0:NT * NE].rearrange("p (t e) -> p t e", t=NT), E[k], ALU.mult)
                    op(v.tensor_reduce(rank[:, c], prod, AX.X, ALU.add))
                    tt(prod, ovs[:, 2:3, :].broadcast_to([P, NT, NE]), E[k], ALU.mult)
                    op(v.tensor_reduce(base[:, c], prod, AX.X, ALU.add))
                    ts(expert[:, c], r9[:, :, 3 + 2 * k], -1.0, float(NE), ALU.mult, ALU.add)
                ri = rki[:, 0:2 * NT]
                op(v.tensor_copy(ri, rank))
                ts(ri, ri, 7, None, ALU.logical_shift_right)
                op(v.tensor_copy(hi, ri))
                op(v.scalar_tensor_tensor(lo, hi, -128.0, rank, ALU.mult, ALU.add))
                ts(low, hi, 1.0, None, ALU.min)
                tt(base, base, hi, ALU.add)
                tt(base, base, expert, ALU.subtract)
                op(v.scalar_tensor_tensor(base, base, float(NE - 1), low, ALU.add, ALU.mult))
                tt(col, base, expert, ALU.add)
                for k in range(2):
                    c = slice(k * NT, (k + 1) * NT)
                    tt(col[:, c], col[:, c], valid[:], ALU.mult)
                    op(v.scalar_tensor_tensor(col[:, c], valid[:], -1.0, col[:, c], ALU.add, ALU.add))
                for k in range(2):
                    c = slice(k * NT, (k + 1) * NT)
                    step.mark(v.tensor_tensor(slot_of[:, c], iota[:].unsqueeze(1).broadcast_to([P, NT, P]),
                                              lo[:, c].unsqueeze(2).broadcast_to([P, NT, P]), ALU.is_equal))
                    in_block = block_of[:, c, 0:NBLK]
                    tt(in_block, iota[:, 0:NBLK].unsqueeze(1).broadcast_to([P, NT, NBLK]),
                       col[:, c].unsqueeze(2).broadcast_to([P, NT, NBLK]), ALU.is_equal)
                    for q, w in ((2, gate), (1, kscale), (0, tokens1)):
                        ins = v.tensor_tensor(block_of[:, c, q * NBLK:(q + 1) * NBLK], in_block,
                                              w[:, c].unsqueeze(2).broadcast_to([P, NT, NBLK]), ALU.mult)
                        if q:
                            step.link(ins)
                    ins.then_inc(s["rk_r"], 1)
                dve.wait_ge(s["rk_inv"], BASE + l + 1)
                op(v.tensor_copy(inv[:].rearrange("p q n -> p (q n)"), ps[:, 0, 0:3 * NBLK]))
                skip, row = prod[:, 0:2, :].rearrange("p a b -> p (a b)")[:, 0:NBLK], tmp[:, 0:2, :].rearrange("p a b -> p (a b)")[:, 0:NBLK]
                ts(skip, inv[:, 0], 0.0, float(SKIP), ALU.is_equal, ALU.mult)
                op(v.scalar_tensor_tensor(row, inv[:, 0], -1.0, skip, ALU.add, ALU.add))
                op(v.tensor_copy(gidx[:], row))
                op(v.scalar_tensor_tensor(row, inv[:, 1], float(T), row, ALU.mult, ALU.add))
                v.tensor_copy(sidx[:], row).then_inc(s["idx_ready"], 1)

                def xg_evict(e, slot):
                    n = NE * l + e
                    dve.wait_ge(s["xg_mm"], BASE + n + 3)
                    dve.wait_ge(s["gu_mm"], BASE + 2 * n + 2)
                    v.tensor_copy(xgT[:, slot, 4:8].rearrange("p k t -> p (k t)"), ps[:, 1, :]).then_inc(s["xg_d"], 1)

                def hidden(e, slot):
                    n = NE * l + e
                    dve.wait_ge(s["dn_mm"], BASE + n + 1)
                    for q in range(2):
                        dve.wait_ge(s["silu"], BASE + 2 * n + q + 1)
                        v.tensor_tensor(hT[:, slot, 2 * q:2 * q + 2].rearrange("p f t -> p (f t)"),
                                        ps[:, 2 + 2 * slot + q, 2 * P:4 * P],
                                        sg[:, 2 * q:2 * q + 2].rearrange("p f t -> p (f t)"), ALU.mult
                                        ).then_inc(s["h_ready"], 1)

                def y_evict(e, slot, turn):
                    n = NE * l + e
                    dve.wait_ge(s["dn_mm"], BASE + n + 3)
                    dve.wait_ge(s["ys_free"], BASE + n + 1)
                    v.tensor_scalar(ys[:, slot, 512:DM], ps[:, 7, :], inv[:, 2, ds(e, 1)], None, ALU.mult
                                    ).then_inc(s["y_d"], 1)

                xg_evict(0, 0)
                settle(dve, s["dve_passed"])
                with dve.Fori(0, NE // 2 - 1) as i:
                    hidden(2 * i, 0)
                    xg_evict(2 * i + 1, 1)
                    y_evict(2 * i, 0, i)
                    hidden(2 * i + 1, 1)
                    xg_evict(2 * i + 2, 0)
                    y_evict(2 * i + 1, 1, i)
                i = NE // 2 - 1
                hidden(2 * i, 0)
                xg_evict(2 * i + 1, 1)
                y_evict(2 * i, 0, i)
                hidden(2 * i + 1, 1)
                y_evict(2 * i + 1, 1, i)

                settle(dve, s["dve_passed"])
                with dve.If(dve.value_load(over[0:1, OVER:OVER + 1], min_val=0, max_val=OVER) > 0):
                    settle(dve, s["dve_passed"])
                    with dve.Fori(0, OVER) as o:
                        n = OVER * l + o
                        dve.wait_ge(s["ov_silu"], BASE + n + 1)
                        v.tensor_tensor(hT[:, 0].rearrange("p f t -> p (f t)"), ps[:, 4, :],
                                        sg.rearrange("p f t -> p (f t)"), ALU.mult).then_inc(s["ov_h"], 1)
                        dve.wait_ge(s["ov_dn"], BASE + n + 1)
                        v.tensor_scalar(ys[:, 0], ps[:, 6:8, :].rearrange("p a b -> p (a b)"),
                                        inv[:, 2, ds(o + NE, 1)], None, ALU.mult).then_inc(s["ov_y"], 1)
                with dve.Else():
                    dve.sem_inc(s["ov_h"], OVER)
                    dve.sem_inc(s["ov_y"], OVER)

                def add2(t, slot, rows, turn):
                    m = NT * l + t
                    dve.wait_ge(s[f"l2_in{slot}"], BASE + 48 * ((5 - slot) * l + turn + 1))
                    tv = t2_of(t, rows)
                    step.link(v.scalar_tensor_tensor(tv, l2in[0:rows, slot, 2 * DM:], ALPHA, l2in[0:rows, slot, 0:DM],
                                                     ALU.mult, ALU.add))
                    v.tensor_tensor(tv, tv, l2in[0:rows, slot, DM:2 * DM], ALU.add).then_inc(s["l2_add"], 1)
                    dve.wait_ge(s["l2_add"], BASE + m + 1)
                    settle(dve, s["dve_passed"])
                    moments(tv, slot, rows, s["l2_stat"])

                def scaled2(t, slot, rows):
                    dve.wait_ge(s["l2_hat"], BASE + NT * l + t + 1)
                    v.tensor_tensor(t2_of(t, rows), t2_of(t, rows), lnp[0:rows, 2], ALU.mult
                                    ).then_inc(s["l2_scaled"], 1)

                add2(0, 0, P, 0)
                add2(1, 1, P, 0)
                scaled2(0, 0, P)
                settle(dve, s["dve_passed"])
                with step.loop(3, 6) as i:
                    for slot in range(2):
                        add2(2 * i + slot + 2, slot, P, i + 1)
                        scaled2(2 * i + slot + 1, 1 - slot, P)
                        xt_evict(NT * (l + 1) + 2 * i + slot, slot, (2 * i + slot) * P, P)
                add2(8, 0, NS, 4)
                scaled2(7, 1, P)
                xt_evict(NT * (l + 1) + 6, 0, 6 * P, P)
                scaled2(8, 0, NS)
                xt_evict(NT * (l + 1) + 7, 1, 7 * P, P)
                xt_evict(NT * (l + 1) + 8, 0, SEQ, NS)

        @block.gpsimd
        def _(pool):
            raise_to_base(pool, "gpsimd")
            g = nc.gpsimd
            step = Steps(pool, s["pool_step"], s["pool_passed"])
            pool.wait_ge(s["const_in"], BASE + 16 * N_CONST)
            pool.wait_ge(s["init"], BASE + 6)

            def inverse_std(rows, slot, done):
                r = slice(0, rows)
                step.link(g.tensor_scalar(rstd[r, slot, 1:2], mv[r, slot, 1:2], EPS, None, ALU.add))
                step.link(g.tensor_tensor(rstd[r, slot, 0:1], rstd[r, slot, 1:2], mhalf[r], ALU.pow))
                step.link(g.tensor_tensor(rstd[r, slot, 1:2], mv[r, slot, 0:1], rstd[r, slot, 0:1], ALU.mult))
                g.tensor_scalar(rstd[r, slot, 1:2], rstd[r, slot, 1:2], -1.0, None, ALU.mult).then_inc(done, 1)

            with step.loop(DEPTH, STEPS_POOL) as l:
                for r in range(5):
                    for ch in range(NCH):
                        cols = slice(ch * CH, (ch + 1) * CH)
                        pool.wait_ge(s["act_ev"], BASE + (l * NTILE + r) * NCH + ch + 1 + 6)
                        g.tensor_tensor(zT[:, r, cols], ztmp[:, r % 2, cols], cosT[:, cols], ALU.mult
                                        ).then_inc(s["cos_done"], 1)
                pool.wait_ge(s["state_in"], BASE + 16 * (l + 1))
                settle(pool, s["pool_passed"])
                g.tensor_copy(su[:, :, 0:2], st[:]).then_inc(s["state_set"], 1)

                pool.wait_ge(s["conv_done"], BASE + CG * (l + 1))
                pool.wait_ge(s["rope_done"], BASE + 15 * (l + 1))
                pool.wait_ge(s["act_ev"], BASE + (l + 1) * NTILE * NCH + 6)

                def stage(b, slot):
                    n = NB * l + b
                    pool.wait_ge(s["s_mm"], BASE + 2 * n)
                    settle(pool, s["pool_passed"])
                    step.mark(g.tensor_copy(qs[:, slot], zT[:, 1:5, ds(b * P, P)]))
                    step.mark(g.tensor_copy(kwin[:, slot * P:(slot + 1) * P], zT[:, 0, ds(b * P, P)]))
                    step.link(g.tensor_copy(vs, zT[:, 5, ds(b * P, P)]))
                    pool.sem_inc(s["stage_done"], 1)

                def stage_gate(b, slot, cols):
                    m = NT * l + b
                    pool.wait_ge(s["wo_mm"], BASE + m + 1)
                    settle(pool, s["pool_passed"])
                    g.tensor_copy(mixT[:, slot, 4:8, 0:cols], gT[:, :, ds(b * P, cols)]).then_inc(s["gate_staged"], 1)

                def inverse1(b, rows):
                    pool.wait_ge(s["ln_stat"], BASE + NT * l + b + 1)
                    settle(pool, s["pool_passed"])
                    inverse_std(rows, 0, s["ln_rstd"])

                pool.wait_ge(s["lnp_in"], BASE + 16 * (l + 1))
                stage(0, 0)
                stage_gate(0, 0, P)

                pool.wait_ge(s["smp_in"], BASE + 32 * (l + 1))
                settle(pool, s["pool_passed"])
                step.mark(g.memset(ptz, 0.0))
                step.mark(g.tensor_copy(kTs[:, :, P], zT[:, 0, SEQ:T]))
                step.link(g.memset(qz, 0.0))
                for h in range(NKV):
                    ins = g.tensor_copy(
                        qz[h * HD:(h + 1) * HD].rearrange("p (b x) -> p b x", b=NS)[:, :, h * QPK:(h + 1) * QPK],
                        zT[h * HD:(h + 1) * HD, 1:5, SEQ:T].rearrange("p j b -> p b j"))
                    step.link(ins)
                pool.sem_inc(s["smp_q"], 1)

                stage(1, 1)
                with step.loop(3, 2 * 6) as i:
                    for n in range(2):
                        stage(2 * i + n + 2, n)
                        stage_gate(2 * i + n + 1, 1 - n, P)
                        inverse1(2 * i + n, P)
                stage_gate(7, 1, P)
                inverse1(6, P)
                stage_gate(8, 0, NS)
                inverse1(7, P)
                inverse1(8, NS)

                def gather(e, slot, turn):
                    n = NE * l + e
                    pool.wait_ge(s["xg_mm"], BASE + n + 1)
                    settle(pool, s["pool_passed"])
                    step.link(g.tensor_copy(gcol[:, slot:slot + 1], gidx[:, ds(e, 1)]))
                    g.indirect_dma_start(out=xg[:, slot], out_offset=None, in_=a["xs1"],
                                         in_offset=bass.IndirectOffsetOnAxis(ap=gcol[:, slot:slot + 1], axis=0),
                                         bounds_check=T - 1, oob_is_err=False).then_inc(s[f"xg_in{slot}"], 16)

                def scatter(e, slot, turn):
                    n = NE * l + e
                    if turn is not None:
                        pool.wait_ge(s[f"sc_out{slot}"], 16 * (NE // 2 * l + turn))
                        settle(pool, s["pool_passed"])
                    step.link(g.tensor_copy(scol[:, slot:slot + 1], sidx[:, ds(e, 1)]))
                    pool.sem_inc(s["ys_free"], 1)
                    pool.wait_ge(s["y_a"], BASE + n + 1)
                    pool.wait_ge(s["y_d"], BASE + n + 1)
                    settle(pool, s["pool_passed"])
                    g.indirect_dma_start(out=a["ytok"].rearrange("k t d -> (k t) d"),
                                         out_offset=bass.IndirectOffsetOnAxis(ap=scol[:, slot:slot + 1], axis=0),
                                         in_=ys[:, slot], in_offset=None,
                                         bounds_check=2 * T - 1, oob_is_err=False).then_inc(s[f"sc_out{slot}"], 16)

                pool.wait_ge(s["idx_ready"], BASE + l + 1)
                pool.wait_ge(s["x1_out0"], BASE + 16 * 5 * (l + 1))
                pool.wait_ge(s["x1_out1"], BASE + 16 * 4 * (l + 1))
                pool.wait_ge(s["smp_mix"], BASE + l + 1)
                pool.wait_ge(s["wo_mm"], BASE + NT * (l + 1) + 2)
                gather(0, 0, 0)
                gather(1, 1, 0)
                for slot in range(2):
                    scatter(slot, slot, None)
                    gather(slot + 2, slot, 1)
                with step.loop(NE // 2 - 2, 4) as i:
                    for slot in range(2):
                        scatter(2 * i + slot + 2, slot, i + 1)
                        gather(2 * i + slot + 4, slot, i + 2)
                for slot in range(2):
                    scatter(NE - 2 + slot, slot, NE // 2 - 1)

                settle(pool, s["pool_passed"])
                with pool.If(pool.value_load(over[0:1, OVER:OVER + 1], min_val=0, max_val=OVER) > 0):
                    pool.wait_ge(s["xg_mm"], BASE + NE * (l + 1) + 2)
                    for slot in range(2):
                        pool.wait_ge(s[f"sc_out{slot}"], 16 * (NE // 2) * (l + 1))
                    settle(pool, s["pool_passed"])
                    before = pool.value_load(over[0:1, OVER + 1:OVER + 2], min_val=0, max_val=DEPTH - 1)
                    with pool.Fori(0, OVER) as o:
                        n = OVER * l + o
                        sent = 16 * (OVER * before + o + 1)
                        pool.wait_ge(s["ov_xt"], BASE + n)
                        settle(pool, s["pool_passed"])
                        g.tensor_copy(gcol[:, 0:1], gidx[:, ds(o + NE, 1)]).then_inc(s["ov_col"], 1)
                        g.tensor_copy(scol[:, 0:1], sidx[:, ds(o + NE, 1)]).then_inc(s["ov_col"], 1)
                        pool.wait_ge(s["ov_col"], BASE + 2 * (n + 1))
                        settle(pool, s["pool_passed"])
                        g.indirect_dma_start(out=xg[:, 0], out_offset=None, in_=a["xs1"],
                                             in_offset=bass.IndirectOffsetOnAxis(ap=gcol[:, 0:1], axis=0),
                                             bounds_check=T - 1, oob_is_err=False).then_inc(s["ov_x"], 16)
                        pool.wait_ge(s["ov_x"], sent)
                        pool.sem_inc(s["ov_xin"], 1)
                        pool.wait_ge(s["ov_y"], BASE + n + 1)
                        settle(pool, s["pool_passed"])
                        g.indirect_dma_start(out=a["ytok"].rearrange("k t d -> (k t) d"),
                                             out_offset=bass.IndirectOffsetOnAxis(ap=scol[:, 0:1], axis=0),
                                             in_=ys[:, 0], in_offset=None,
                                             bounds_check=2 * T - 1, oob_is_err=False).then_inc(s["ov_sc"], 16)
                        pool.wait_ge(s["ov_sc"], sent)
                        pool.sem_inc(s["ov_out"], 1)
                with pool.Else():
                    pool.sem_inc(s["ov_col"], 2 * OVER)
                    pool.sem_inc(s["ov_xin"], OVER)
                    pool.sem_inc(s["ov_out"], OVER)

                def inverse2(t, slot, rows):
                    pool.wait_ge(s["l2_stat"], BASE + NT * l + t + 1)
                    settle(pool, s["pool_passed"])
                    inverse_std(rows, slot, s["l2_rstd"])

                def finish2(t, slot, rows, turn):
                    pool.wait_ge(s["l2_scaled"], BASE + NT * l + t + 1)
                    pool.wait_ge(s["xt_mm"], BASE + NT * (l + 1) + t + 1)
                    pool.wait_ge(s[f"x2_out{slot}"], BASE + 16 * ((5 - slot) * l + turn))
                    g.tensor_tensor(x2[0:rows, slot], t2_of(t, rows), lnp[0:rows, 3], ALU.add).then_inc(s["x2_ready"], 1)

                inverse2(0, 0, P)
                with step.loop(3, 6) as i:
                    for slot in range(2):
                        inverse2(2 * i + slot + 1, 1 - slot, P)
                        finish2(2 * i + slot, slot, P, i)
                inverse2(7, 1, P)
                finish2(6, 0, P, 3)
                inverse2(8, 0, NS)
                finish2(7, 1, P, 3)
                finish2(8, 0, NS, 4)


def kernel(**inputs):
    import numpy as _np
    import concourse.bacc as _bacc
    from concourse.bass_utils import run_bass_kernel_spmd as _run

    f = {n: _np.asarray(v) for n, v in inputs.items()}
    L = DEPTH
    f32 = _np.float32
    A, KV, C = NH * HD, NKV * HD, CG * P
    cols = [_np.arange(A, A + KV)]
    for j in range(QPK):
        cols.append(_np.concatenate([_np.arange(h * HD, (h + 1) * HD) for h in (j, j + QPK)]))
    cols.append(_np.arange(A + KV, A + 2 * KV))
    at_b, at_c, at_h = A + 2 * KV, A + 2 * KV + C, A + 2 * KV + 2 * C
    for g in range(CG):
        cols += [_np.arange(o + g * P, o + (g + 1) * P) for o in (at_c, at_h, at_b)]
    w_in = f["w_in"][:, :, _np.concatenate(cols)].reshape(L, KD, P, NTILE, P).transpose(0, 3, 2, 1, 4)

    pos = _np.concatenate([_np.arange(SEQ), _np.full(NS, PAST)]).astype(f32)
    freq = (10000.0 ** (-_np.arange(HD // 2) / (HD // 2))).astype(f32)
    ang = (pos[None, :] * freq[_np.arange(P) % (HD // 2)][:, None]).astype(f32)
    swap = _np.zeros((P, P), f32)
    for m in range(P):
        d = m % HD
        swap[(m + HD // 2) if d < HD // 2 else (m - HD // 2), m] = -1.0 if d < HD // 2 else 1.0
    q_at, k_at = _np.arange(P)[:, None], _np.arange(P)[None, :]
    cur = _np.where(k_at <= q_at, 0.0, -BIG)
    prev = _np.where(k_at >= q_at, 0.0, -BIG)
    none = _np.full((P, P), -BIG)
    masks = _np.stack([_np.concatenate(m, 1) for m in ((cur, none), (cur, prev), (prev, cur))], 1)
    tok = _np.arange(NT)[None, :] * P + _np.arange(P)[:, None]
    arrays = {
        "x_all": _np.concatenate([f["x_prompt"].reshape(SEQ, DM), f["x_sample"].reshape(NS, DM)]),
        "w_in": w_in.reshape(L * NTILE, P, DM),
        "w_o": f["w_o"],
        "sinks": f["attn_sinks"].reshape(-1),
        "sinkc": _np.tile(f["attn_sinks"], (1, NS)).T,
        "conv_w": f["conv_w"].reshape(L, 3, CG, P).transpose(3, 0, 2, 1),
        "ln": _np.stack([f[n] for n in ("ln1_g", "ln1_b", "ln2_g", "ln2_b")], 1).reshape(L, 4 * DM),
        "w_r": _np.concatenate([f["w_router_group"], f["w_router_expert"]], 2),
        "b_r": _np.concatenate([f["b_router_group"], f["b_router_expert"]], 1),
        "w_gate": f["w_gate"], "w_up": f["w_up"], "w_down": f["w_down"],
        "cache_kT": f["cache_k_win"].reshape(L, NS, P, P).transpose(0, 3, 1, 2),
        "cache_v": f["cache_v_win"].reshape(L, NS, P, P),
        "state": f["state_conv"].reshape(L, NS, 2, CG, P).transpose(0, 4, 3, 1, 2).reshape(L, P, CG * NS, 2),
        "c_ident": _np.eye(P, dtype=f32),
        "c_rot": swap,
        "c_upper": _np.triu(_np.ones((P, P), f32), 1),
        "c_iota": _np.tile(_np.arange(P, dtype=f32), (P, 1)),
        "c_masks": masks.astype(f32),
        "c_cos": _np.cos(ang), "c_sin": _np.sin(ang),
        "c_desc": _np.tile(_np.arange(NE, 0, -1, dtype=f32), (P, 1)),
        "c_tok1": _np.tile(tok + 1, (1, 2)).astype(f32),
        "c_k": _np.tile(_np.repeat(_np.arange(2, dtype=f32), NT), (P, 1)),
        "c_valid": (tok < T).astype(f32),
        "c_sel8": _np.repeat(_np.eye(NS, dtype=f32), NH, 0),
        "c_half": _np.stack([_np.arange(64) % NH < QPK, _np.arange(64) % NH >= QPK], 1).astype(f32),
    }
    outs = {
        "y_all": (L + 1, T, DM), "o_kp": (L, P, P), "o_vp": (L, P, P), "o_ks": (L, P, NS, P),
        "o_vs": (L, NS, P, P), "o_cp": (L, P, CG, 2), "o_cs": (L, P, CG * NS, 3),
    }
    nc = _bacc.Bacc("TRN2", target_bir_lowering=False, num_devices=1)
    aps, feed = {}, {}
    for name, v in arrays.items():
        feed[f"in_{name}"] = v = _np.ascontiguousarray(v)
        aps[name] = nc.dram_tensor(f"in_{name}", v.shape, mybir.dt.from_np(v.dtype), kind="ExternalInput").ap()
    for name, shape in outs.items():
        aps[name] = nc.dram_tensor(f"out_{name}", shape, F32, kind="ExternalOutput").ap()
    aps["xs1"] = nc.dram_tensor("xs1", (T, DM), F32).ap()
    aps["ytok"] = nc.dram_tensor("ytok", (2, T, DM), F32).ap()
    build(nc, aps)
    r = _run(nc, [feed], core_ids=[0]).results[0]
    o = {name: r[f"out_{name}"] for name in outs}

    def windows(t):
        return _np.ascontiguousarray(t.transpose(0, 2, 1)).reshape(L, 1, P, NKV, HD)

    y = o["y_all"][L]
    return (
        y[:SEQ].reshape(1, SEQ, DM), y[SEQ:].reshape(NS, 1, DM), windows(o["o_kp"]), windows(o["o_vp"]),
        _np.ascontiguousarray(o["o_cp"].transpose(0, 3, 2, 1)).reshape(L, 1, 2, C),
        _np.ascontiguousarray(o["o_ks"].transpose(0, 2, 3, 1)).reshape(L, NS, P, NKV, HD),
        o["o_vs"].reshape(L, NS, P, NKV, HD),
        _np.ascontiguousarray(o["o_cs"].reshape(L, P, CG, NS, 3)[..., 1:].transpose(0, 3, 4, 2, 1)).reshape(L, NS, 2, C),
    )
```
